# Optimizing a Trainium2 kernel written in Bass

```python
import math
import jax, jax.numpy as jnp
from jax import lax
import numpy as np

D_MODEL = 1024
BATCH = 1
SEQ = 512
DEPTH = 2
DEC_BATCH = 8
DEC_SEQ = 8
PAST_LEN = 2048
PAGE_SIZE = 128

N_MIXERS = 2
N_MLSTM = (DEPTH + 1) // 2
N_SWA = DEPTH // 2
MLSTM_HEADS = 4
MLSTM_DV = D_MODEL // MLSTM_HEADS
MLSTM_DK = MLSTM_DV // 2
MLSTM_CHUNK = 64
SWA_HEAD_DIM = 64
SWA_HEADS = D_MODEL // SWA_HEAD_DIM
SWA_KV_HEADS = 4
SWA_GROUP = SWA_HEADS // SWA_KV_HEADS
WINDOW = 128
ROT_DIM = SWA_HEAD_DIM // 4
ROPE_THETA = 500000.0
D_FF = 2816
CONV_W = 3
EPS = 1e-6

kernel_name = 'hybrid_mlstm_swa_convglu_step'

def rmsnorm(x, w):
    xf = x.astype(jnp.float32)
    y = xf * lax.rsqrt(jnp.mean(xf * xf, axis=-1, keepdims=True) + EPS)
    return (y * w.astype(jnp.float32)).astype(x.dtype)

def rope_partial(x, pos):
    half = ROT_DIM // 2
    inv = ROPE_THETA ** (-jnp.arange(half, dtype=jnp.float32) * 2.0 / ROT_DIM)
    ang = pos[:, None] * inv[None, :]
    cos = jnp.cos(ang)[:, None, :]
    sin = jnp.sin(ang)[:, None, :]
    x1 = x[..., :half]
    x2 = x[..., half:ROT_DIM]
    return jnp.concatenate([x1 * cos - x2 * sin, x2 * cos + x1 * sin, x[..., ROT_DIM:]], axis=-1)

def mlstm_chunkwise(q, k, v, logi, logf, C0, n0, m0):
    B, T, H, _ = q.shape
    DV = v.shape[-1]
    L = math.gcd(T, MLSTM_CHUNK)
    nc = T // L

    def to_chunks(x):
        x = x.astype(jnp.float32).reshape((B, nc, L, H) + x.shape[3:])
        return jnp.moveaxis(x, (1, 3), (0, 2))

    causal = jnp.tril(jnp.ones((L, L), dtype=bool))

    def step(carry, inp):
        C, n, m = carry
        qc, kc, vc, ic, fc = inp
        b = jnp.cumsum(fc, axis=-1)
        d = b[..., :, None] - b[..., None, :] + ic[..., None, :]
        d = jnp.where(causal, d, -jnp.inf)
        m_inter = b + m[..., None]
        m_t = jnp.maximum(m_inter, d.max(-1))
        w_intra = jnp.exp(d - m_t[..., None]) * jnp.einsum('bhtd,bhsd->bhts', qc, kc)
        w_inter = jnp.exp(m_inter - m_t)
        num = w_inter[..., None] * jnp.einsum('bhtd,bhde->bhte', qc, C) + jnp.einsum('bhts,bhse->bhte', w_intra, vc)
        nq = w_inter * jnp.einsum('bhtd,bhd->bht', qc, n) + w_intra.sum(-1)
        h = num / jnp.maximum(jnp.abs(nq), jnp.exp(-m_t))[..., None]
        m_new = m_t[..., -1]
        w_state = jnp.exp(b[..., -1:] - b + ic - m_new[..., None])
        decay = jnp.exp(b[..., -1] + m - m_new)
        C_new = decay[..., None, None] * C + jnp.einsum('bhs,bhsd,bhse->bhde', w_state, kc, vc)
        n_new = decay[..., None] * n + jnp.einsum('bhs,bhsd->bhd', w_state, kc)
        return (C_new, n_new, m_new), h

    carry0 = (C0.astype(jnp.float32), n0.astype(jnp.float32), m0.astype(jnp.float32))
    (C, n, m), hs = lax.scan(step, carry0, (to_chunks(q), to_chunks(k), to_chunks(v), to_chunks(logi), to_chunks(logf)))
    hs = hs.transpose(1, 0, 3, 2, 4).reshape(B, T, H, DV)
    return hs, C, n, m

def mlstm_mixer(h, C0, n0, m0, w_in, b_gates, head_norm, w_out):
    B, T, _ = h.shape
    HK = MLSTM_HEADS * MLSTM_DK
    HV = MLSTM_HEADS * MLSTM_DV
    proj = h @ w_in
    q = proj[..., :HK].reshape(B, T, MLSTM_HEADS, MLSTM_DK)
    k = proj[..., HK:2 * HK].reshape(B, T, MLSTM_HEADS, MLSTM_DK) * (MLSTM_DK ** -0.5)
    v = proj[..., 2 * HK:2 * HK + HV].reshape(B, T, MLSTM_HEADS, MLSTM_DV)
    o = proj[..., 2 * HK + HV:2 * HK + 2 * HV]
    g = proj[..., 2 * HK + 2 * HV:].astype(jnp.float32) + b_gates.astype(jnp.float32)
    logi = g[..., :MLSTM_HEADS]
    logf = jax.nn.log_sigmoid(g[..., MLSTM_HEADS:])
    hs, C, n, m = mlstm_chunkwise(q, k, v, logi, logf, C0, n0, m0)
    hn = hs * lax.rsqrt(jnp.mean(hs * hs, axis=-1, keepdims=True) + EPS)
    hn = hn.reshape(B, T, HV) * head_norm.astype(jnp.float32)
    y = (hn.astype(h.dtype) * jax.nn.sigmoid(o)) @ w_out
    return y, C.astype(C0.dtype), n.astype(n0.dtype), m.astype(m0.dtype)

def swa_qkv(h, pos, w_qkv, q_norm, k_norm):
    B, T, _ = h.shape
    HQ = SWA_HEADS * SWA_HEAD_DIM
    HKV = SWA_KV_HEADS * SWA_HEAD_DIM
    proj = h @ w_qkv
    q = proj[..., :HQ].reshape(B, T, SWA_HEADS, SWA_HEAD_DIM)
    k = proj[..., HQ:HQ + HKV].reshape(B, T, SWA_KV_HEADS, SWA_HEAD_DIM)
    v = proj[..., HQ + HKV:].reshape(B, T, SWA_KV_HEADS, SWA_HEAD_DIM)
    q = rope_partial(rmsnorm(q, q_norm).astype(jnp.float32), pos).astype(h.dtype)
    k = rope_partial(rmsnorm(k, k_norm).astype(jnp.float32), pos).astype(h.dtype)
    return q, k, v

def swa_attend(q, k, v, mask, sinks):
    qg = q.reshape(q.shape[:-2] + (SWA_KV_HEADS, SWA_GROUP, SWA_HEAD_DIM))
    s = jnp.einsum('...qkgd,...skd->...kgqs', qg, k, preferred_element_type=jnp.float32) * (SWA_HEAD_DIM ** -0.5)
    s = jnp.where(mask[..., None, None, :, :], s, -jnp.inf)
    sink = sinks.astype(jnp.float32).reshape(SWA_KV_HEADS, SWA_GROUP, 1, 1)
    m = jnp.maximum(s.max(-1, keepdims=True), sink)
    p = jnp.exp(s - m)
    denom = p.sum(-1, keepdims=True) + jnp.exp(sink - m)
    o = jnp.einsum('...kgqs,...skd->...qkgd', (p / denom).astype(v.dtype), v)
    return o.reshape(q.shape)

def swa_prompt(h, w_qkv, q_norm, k_norm, sinks, w_out):
    B, T, _ = h.shape
    q, k, v = swa_qkv(h, jnp.arange(T, dtype=jnp.float32), w_qkv, q_norm, k_norm)
    nb = T // WINDOW
    qb = q.reshape(B, nb, WINDOW, SWA_HEADS, SWA_HEAD_DIM)

    def band(x):
        xb = x.reshape(B, nb, WINDOW, SWA_KV_HEADS, SWA_HEAD_DIM)
        prev = jnp.concatenate([jnp.zeros_like(xb[:, :1]), xb[:, :-1]], axis=1)
        return jnp.concatenate([prev, xb], axis=2)

    blk = jnp.arange(nb)[:, None]
    qpos = blk * WINDOW + jnp.arange(WINDOW)[None, :]
    kpos = (blk - 1) * WINDOW + jnp.arange(2 * WINDOW)[None, :]
    rel = qpos[:, :, None] - kpos[:, None, :]
    mask = (rel >= 0) & (rel <= WINDOW) & (kpos[:, None, :] >= 0)
    o = swa_attend(qb, band(k), band(v), mask, sinks).reshape(B, T, SWA_HEADS * SWA_HEAD_DIM)
    return o @ w_out, k[:, T - WINDOW:], v[:, T - WINDOW:]

def swa_sample(h, k_buf, v_buf, w_qkv, q_norm, k_norm, sinks, w_out):
    B, T, _ = h.shape
    W = k_buf.shape[1]
    q, k, v = swa_qkv(h, PAST_LEN + jnp.arange(T, dtype=jnp.float32), w_qkv, q_norm, k_norm)
    k_all = jnp.concatenate([k_buf.astype(k.dtype), k], axis=1)
    v_all = jnp.concatenate([v_buf.astype(v.dtype), v], axis=1)
    qpos = PAST_LEN + jnp.arange(T)
    kpos = PAST_LEN - W + jnp.arange(W + T)
    rel = qpos[:, None] - kpos[None, :]
    mask = (rel >= 0) & (rel <= WINDOW)
    o = swa_attend(q, k_all, v_all, mask, sinks).reshape(B, T, SWA_HEADS * SWA_HEAD_DIM)
    return o @ w_out, k_all[:, T:], v_all[:, T:]

def conv_glu(h, conv_buf, w_up, conv_w, conv_b, w_down):
    B, T, _ = h.shape
    up = h @ w_up
    g = up[..., :D_FF]
    u = up[..., D_FF:]
    gp = jnp.concatenate([conv_buf.astype(g.dtype), g], axis=1)
    gc = conv_b
    for j in range(CONV_W):
        gc = gc + conv_w[j] * gp[:, j:j + T]
    y = (jax.nn.gelu(gc, approximate=False) * u) @ w_down
    return y, gp[:, T:]

def setup_inputs(seed: int = 0) -> dict:
    key = jax.random.key(seed)
    ks = jax.random.split(key, 24)
    f32 = jnp.float32
    nrm = lambda k, shape, s: jax.random.normal(k, shape, f32) * s
    w_buf = min(WINDOW, PAST_LEN)
    mlstm_in_width = 2 * MLSTM_HEADS * MLSTM_DK + 2 * MLSTM_HEADS * MLSTM_DV + 2 * MLSTM_HEADS
    swa_in_width = (SWA_HEADS + 2 * SWA_KV_HEADS) * SWA_HEAD_DIM
    b_gates = jnp.concatenate([
        nrm(ks[0], (N_MLSTM, MLSTM_HEADS), 0.1),
        3.0 + nrm(ks[1], (N_MLSTM, MLSTM_HEADS), 0.1)], axis=-1)
    return {
        'x_prompt': nrm(ks[2], (BATCH, SEQ, D_MODEL), 1.0),
        'x_sample': nrm(ks[3], (DEC_BATCH, DEC_SEQ, D_MODEL), 1.0),
        'state_mlstm_C': nrm(ks[4], (N_MLSTM, DEC_BATCH, MLSTM_HEADS, MLSTM_DK, MLSTM_DV), 0.1),
        'state_mlstm_n': nrm(ks[5], (N_MLSTM, DEC_BATCH, MLSTM_HEADS, MLSTM_DK), 0.5),
        'state_mlstm_m': nrm(ks[6], (N_MLSTM, DEC_BATCH, MLSTM_HEADS), 1.0),
        'cache_swa_k': nrm(ks[7], (N_SWA, DEC_BATCH, w_buf, SWA_KV_HEADS, SWA_HEAD_DIM), 1.0),
        'cache_swa_v': nrm(ks[8], (N_SWA, DEC_BATCH, w_buf, SWA_KV_HEADS, SWA_HEAD_DIM), 1.0),
        'state_ffn_conv': nrm(ks[9], (DEPTH, DEC_BATCH, CONV_W - 1, D_FF), 1.0),
        'norm_mix': 1.0 + nrm(ks[10], (DEPTH, D_MODEL), 0.02),
        'norm_ffn': 1.0 + nrm(ks[11], (DEPTH, D_MODEL), 0.02),
        'w_mlstm_in': nrm(ks[12], (N_MLSTM, D_MODEL, mlstm_in_width), D_MODEL ** -0.5),
        'b_mlstm_gates': b_gates,
        'mlstm_head_norm': 1.0 + nrm(ks[13], (N_MLSTM, MLSTM_HEADS * MLSTM_DV), 0.02),
        'w_mlstm_out': nrm(ks[14], (N_MLSTM, MLSTM_HEADS * MLSTM_DV, D_MODEL), (MLSTM_HEADS * MLSTM_DV) ** -0.5),
        'w_swa_qkv': nrm(ks[15], (N_SWA, D_MODEL, swa_in_width), D_MODEL ** -0.5),
        'swa_q_norm': 1.0 + nrm(ks[16], (N_SWA, SWA_HEAD_DIM), 0.02),
        'swa_k_norm': 1.0 + nrm(ks[17], (N_SWA, SWA_HEAD_DIM), 0.02),
        'swa_sinks': nrm(ks[18], (N_SWA, SWA_HEADS), 0.5),
        'w_swa_out': nrm(ks[19], (N_SWA, SWA_HEADS * SWA_HEAD_DIM, D_MODEL), (SWA_HEADS * SWA_HEAD_DIM) ** -0.5),
        'w_ffn_up': nrm(ks[20], (DEPTH, D_MODEL, 2 * D_FF), D_MODEL ** -0.5),
        'ffn_conv_w': nrm(ks[21], (DEPTH, CONV_W, D_FF), CONV_W ** -0.5),
        'ffn_conv_b': nrm(ks[22], (DEPTH, D_FF), 0.02),
        'w_ffn_down': nrm(ks[23], (DEPTH, D_FF, D_MODEL), D_FF ** -0.5),
    }

def reference(x_prompt, x_sample, state_mlstm_C, state_mlstm_n, state_mlstm_m, cache_swa_k, cache_swa_v,
              state_ffn_conv, norm_mix, norm_ffn, w_mlstm_in, b_mlstm_gates, mlstm_head_norm, w_mlstm_out,
              w_swa_qkv, swa_q_norm, swa_k_norm, swa_sinks, w_swa_out, w_ffn_up, ffn_conv_w, ffn_conv_b,
              w_ffn_down):
    xp, xs = x_prompt, x_sample
    B = xp.shape[0]
    dt = xp.dtype
    pC, pn, pm, pk, pv, pconv = [], [], [], [], [], []
    sC, sn, sm, sk, sv, sconv = [], [], [], [], [], []
    for i in range(DEPTH):
        j = i // N_MIXERS
        hp = rmsnorm(xp, norm_mix[i])
        hs = rmsnorm(xs, norm_mix[i])
        if i % N_MIXERS == 0:
            zC = jnp.zeros((B, MLSTM_HEADS, MLSTM_DK, MLSTM_DV), dt)
            zn = jnp.zeros((B, MLSTM_HEADS, MLSTM_DK), dt)
            zm = jnp.zeros((B, MLSTM_HEADS), dt)
            yp, C1, n1, m1 = mlstm_mixer(hp, zC, zn, zm, w_mlstm_in[j], b_mlstm_gates[j], mlstm_head_norm[j], w_mlstm_out[j])
            ys, C2, n2, m2 = mlstm_mixer(hs, state_mlstm_C[j], state_mlstm_n[j], state_mlstm_m[j],
                                         w_mlstm_in[j], b_mlstm_gates[j], mlstm_head_norm[j], w_mlstm_out[j])
            pC.append(C1); pn.append(n1); pm.append(m1)
            sC.append(C2); sn.append(n2); sm.append(m2)
        else:
            yp, k1, v1 = swa_prompt(hp, w_swa_qkv[j], swa_q_norm[j], swa_k_norm[j], swa_sinks[j], w_swa_out[j])
            ys, k2, v2 = swa_sample(hs, cache_swa_k[j], cache_swa_v[j], w_swa_qkv[j], swa_q_norm[j],
                                    swa_k_norm[j], swa_sinks[j], w_swa_out[j])
            pk.append(k1); pv.append(v1)
            sk.append(k2); sv.append(v2)
        xp = xp + yp
        xs = xs + ys
        hp = rmsnorm(xp, norm_ffn[i])
        hs = rmsnorm(xs, norm_ffn[i])
        zconv = jnp.zeros((B, CONV_W - 1, D_FF), dt)
        fp, c1 = conv_glu(hp, zconv, w_ffn_up[i], ffn_conv_w[i], ffn_conv_b[i], w_ffn_down[i])
        fs, c2 = conv_glu(hs, state_ffn_conv[i], w_ffn_up[i], ffn_conv_w[i], ffn_conv_b[i], w_ffn_down[i])
        pconv.append(c1); sconv.append(c2)
        xp = xp + fp
        xs = xs + fs
    return (xp, xs,
            jnp.stack(pC), jnp.stack(pn), jnp.stack(pm), jnp.stack(pk), jnp.stack(pv), jnp.stack(pconv),
            jnp.stack(sC), jnp.stack(sn), jnp.stack(sm), jnp.stack(sk), jnp.stack(sv), jnp.stack(sconv))


_drawn_inputs = setup_inputs


def setup_inputs(seed=0):
    import zlib

    import numpy as np

    out = dict(_drawn_inputs(seed))
    spreads = {}
    factors = {'mlstm_head_norm': 4.544,
     'swa_q_norm': 8.0,
     'swa_k_norm': 2.834,
     'swa_sinks': 64.0,
     'ffn_conv_b': 4.068}
    for name, (base, spread) in spreads.items():
        noise = np.random.default_rng([zlib.crc32(name.encode()), seed]).standard_normal(out[name].shape)
        drawn = base * np.exp(spread * noise) if base else spread * noise
        out[name] = __import__('jax').numpy.asarray(drawn.astype(out[name].dtype))
    for name, factor in factors.items():
        out[name] = (out[name] * factor).astype(out[name].dtype)
    return out
```

```python
import concourse.bass as bass
from concourse import mybir
from contextlib import ExitStack

D = 1024
SEQ = 512
NB, TB = 8, 8
NS = NB * TB
T = SEQ + NS
HALF = T // 2
KD = D // 128
FF = 2816
KF = FF // 128
TT = 5
ROWS = [128, 128, 128, 128, NS]
MH, DK, DV = 4, 128, 256
AH, KVH, HD = 16, 4, 64
WIN = 128
PAST = 2048
EPS = 1e-6
WSCALE = 64.0
NEG = -1.0e30
KEYS = WIN + NS
RING = 4
GC = 2 + SEQ + NB * (2 + TB)
CC = GC - 2
NCO = 2 + NB * 2

SEGS = [("qk", 8), ("v", 8), ("o", 8), ("mout", 8), ("up0", 44), ("down0", 32),
        ("qkv", 12), ("sout", 8), ("up1", 44), ("down1", 32)]
SEG0 = {}
_n = 0
for _name, _count in SEGS:
    SEG0[_name] = _n
    _n += _count
UNITS = _n
DOWN_K = [6, 6, 5, 5]

CONST = [("ident", 128), ("ones", 128), ("sel", 4 * 128), ("cmask", 128), ("bmask", NS), ("blk", NB),
         ("cos", TT * 8), ("sin", TT * 8), ("keep", T), ("drop", T), ("eps", 1),
         ("pmask", 256), ("smask", NB * KEYS)]
COFF = {}
_n = 0
for _name, _count in CONST:
    COFF[_name] = (_n, _n + _count)
    _n += _count
NCONST = _n
NKEPT = COFF["pmask"][0]


def build(nc, I, O):
    f32, f16, bf16 = mybir.dt.float32, mybir.dt.float16, mybir.dt.bfloat16
    ALU, ACT, AX = mybir.AluOpType, mybir.ActivationFunctionType, mybir.AxisListType
    ctx = ExitStack()
    with ctx:
        ctx.enter_context(nc.allow_non_contiguous_dma(reason="small state vectors"))

        def sb(name, shape, dt=f32, into=ctx):
            return into.enter_context(nc.sbuf_tensor(name, shape, dt))

        def sem(name):
            return ctx.enter_context(nc.semaphore(name))

        C = sb("C", [128, NKEPT])
        ident16 = sb("ident16", [128, 128], bf16)
        mask16 = sb("mask16", [128, 256 + NB * KEYS], bf16)
        xT = sb("xT", [128, KD, T])
        hnH = sb("hnH", [128, KD, T], f16)
        hnL = sb("hnL", [128, KD, T], f16)
        stage = sb("stage", [128, RING, 1024])
        wH = sb("wH", [128, RING, 1024], f16)
        wL = sb("wL", [128, RING, 1024], f16)
        pff = sb("pff", [128, KF, 40])
        pd = sb("pd", [128, KD, 5])
        convO = sb("convO", [128, 2, KF, NCO])
        sqsum = sb("sqsum", [128, T])
        sq = sb("sq", [128, T])
        rstd = sb("rstd", [128, T])
        ntmp = sb("ntmp", [128, 2, T])

        def const(name, rows=128):
            a, b = COFF[name]
            return C[0:rows, a:b]

        ident, ones, eps = const("ident"), const("ones"), const("eps")

        masks = hnH[:, :, :].rearrange("p k t -> p (k t)").bitcast(f32)[:, 0:NCONST - NKEPT]

        ph = ExitStack()
        xtok = sb("xtok", [128, TT, D], into=ph)
        rowsF = sb("rowsF", [40, FF], into=ph)
        rowsD = sb("rowsD", [5, D], into=ph)
        sq8 = sb("sq8", [128, KD, T], into=ph)
        ph.close()
        ph = ExitStack()
        qT = sb("qT", [128, MH, T], into=ph)
        kT = sb("kT", [128, MH, T], into=ph)
        vM = sb("vM", [128, TT, MH * DV], into=ph)
        so = sb("so", [128, KD, T], into=ph)
        C0 = sb("C0", [128, 2, NB, DV], into=ph)
        Cp = sb("Cp", [128, 2, DV], into=ph)
        gb = sb("gb", [4, 2], into=ph)
        m0T = sb("m0T", [4, NB], into=ph)
        n0r = sb("n0r", [32, DK], into=ph)
        n0T = sb("n0T", [128, 32], into=ph)
        R = sb("R", [4, 2 * SEQ + 3 * NS], into=ph)
        gcol = sb("gcol", [128, TT, 8], into=ph)
        kw = sb("kw", [128, 4, MH * DK], into=ph)
        kts = sb("kts", [NS, MH * DK], into=ph)
        early = ExitStack()
        gwS = sb("gwS", [128, KD, 64], into=early)
        gwH = sb("gwH", [128, KD, 64], f16, into=early)
        gwL = sb("gwL", [128, KD, 64], f16, into=early)
        FG = sb("FG", [4, T], into=early)
        GL = sb("GL", [4, T], into=early)
        GA2 = sb("GA2", [4, T], into=early)
        GM = sb("GM", [4, T], into=early)
        LI = sb("LI", [4, T], into=early)
        GB = sb("GB", [4, T], into=early)
        WS = sb("WS", [4, T], into=early)
        early.close()
        wbuf = sb("wbuf", [128, 1280 + NS], into=ph)
        dtmp = sb("dtmp", [128, 4 * 128 + NS], into=ph)
        kwm = sb("kwm", [NS, NB, DK], into=ph)
        wsm = sb("wsm", [NS, NB], into=ph)
        wis = sb("wis", [128, 2 * NS], into=ph)
        e1b = sb("e1b", [128, SEQ], into=ph)
        qs = sb("qs", [128, NS], into=ph)
        nqp = sb("nqp", [128, NS], into=ph)
        dec = sb("dec", [128, NB], into=ph)
        nmul = sb("nmul", [128, NB], into=ph)
        nnew = sb("nnew", [128, 36], into=ph)
        nrow = sb("nrow", [36, DK], into=ph)
        hsA = sb("hsA", [128, T], into=ph)
        hsB = sb("hsB", [128, T], into=ph)
        ph.close()
        ph = ExitStack()
        qtok = sb("qtok", [128, TT, 3 * 512], into=ph)
        sqx = sb("sqx", [128, TT, 512], into=ph)
        qTT = sb("qTT", [128, 2, 4, SEQ], into=ph)
        qS = sb("qS", [128, 2, NB, 4 * TB], into=ph)
        kTT = sb("kTT", [128, 2, T], into=ph)
        Kc = sb("Kc", [128, NB, 256], into=ph)
        Vc = sb("Vc", [128, NB, 256], into=ph)
        KcT = sb("KcT", [128, 2, NB, 128], into=ph)
        qw = sb("qw", [128, 2, HD], into=ph)
        sinkb = sb("sinkb", [128, AH], into=ph)
        sinkr = sb("sinkr", [128, 1], into=ph)
        rt = sb("rt", [128, 4, TT, 64], into=ph)
        rss = sb("rss", [128, TT, 8], into=ph)
        P = sb("P", [128, 2, 1024], into=ph)
        PT = sb("PT", [128, 2, 512], into=ph)
        st = sb("st", [128, 2, 6, 4], into=ph)
        ph.close()
        ph = ExitStack()
        hH = sb("hH", [128, KF, T], f16, into=ph)
        hL = sb("hL", [128, KF, T], f16, into=ph)
        G = sb("G", [128, 2, GC], into=ph)
        acc = sb("acc", [128, 2, GC], into=ph)
        h32 = sb("h32", [128, 2, T], into=ph)
        crow = sb("crow", [NCO, 2, FF], into=ph)
        ph.close()
        ph = ExitStack()
        ytok = sb("ytok", [128, TT, D], into=ph)
        ph.close()

        PS = ctx.enter_context(nc.psum_tensor("PS", [128, 8, 512], f32))

        def pair(p):
            return PS[:, 2 * p:2 * p + 2, 0:HALF]

        def halves(ap):
            return ap.rearrange("p (a b) -> p a b", a=2)

        dC, dX, dRows, dGate, dMisc = sem("dC"), sem("dX"), sem("dRows"), sem("dGate"), sem("dMisc")
        staged = [sem(f"staged{i}") for i in range(RING)]
        hi_ready, lo_ready, unit_used = sem("hi_ready"), sem("lo_ready"), sem("unit_used")
        x_tr, x_in = sem("x_tr"), sem("x_in")
        par_tr, par_in = sem("par_tr"), sem("par_in")
        masks_in = sem("masks_in")
        out_done = sem("out_done")
        chA, chV, chP = sem("act_chain"), sem("dve_chain"), sem("pool_chain")
        chains = {"A": 0, "V": 0, "P": 0}

        def link(which, eng, ins):
            s = {"A": chA, "V": chV, "P": chP}[which]
            chains[which] += 1
            ins.then_inc(s, 1)
            eng.wait_ge(s, chains[which])

        nrm = [{s: sem(f"norm{i}_{s}") for s in ("ps", "rs", "tmp", "hi", "lo")} for i in range(4)]
        free = {s: sem(s + "_free") for s in ("qk", "v", "o", "mout", "qkv", "sout", "down0", "down1")}
        tile_done = {s: sem(s + "_tile_done") for s in ("v", "qkv")}
        gsem = {s: sem("gate_" + s) for s in ("w_hi", "w_lo", "ps", "in", "softplus", "scans", "rows", "tr", "cols", "m_out", "kt", "kw", "kts")}
        hsem = {s: sem("head_" + s) for s in ("s", "rows", "e1", "e1b", "dt", "e", "w", "kwm", "num", "cp", "cpi", "cs",
                                              "csi", "abs", "hs", "sq", "ss", "rs", "f", "hi", "lo", "ntr", "nin")}
        dC0 = [sem("dC0a"), sem("dC0b")]
        c_out = [sem("c_outa"), sem("c_outb")]
        asem = {s: sem("attn_" + s) for s in ("rss", "rs", "rope", "tr", "trA", "trV", "s", "m", "e", "p", "t",
                                              "ptA", "ptV", "o", "oh", "ol", "cz", "kz")}
        dKV = sem("dKV")
        ff = [{s: sem(f"ffn{i}_{s}") for s in ("hist", "gate", "tail", "acc", "half", "conv",
                                               "gelu", "h32", "hH", "hL")} for i in range(2)]
        res = {s: (sem(s + "_res_x"), sem(s + "_res_sq")) for s in ("mout", "sout", "down0", "down1")}
        ctr, cin = sem("conv_out_tr"), sem("conv_out_in")
        ytr, yA, yV = sem("y_tr"), sem("y_in_act"), sem("y_in_dve")
        xA, xV, sq_in = sem("x_in_act"), sem("x_in_dve"), sem("x_sq")
        pads = sem("pads")

        block = ctx.enter_context(nc.Block())

        def unit(name, i, u):
            n0 = SEG0[name]
            return n0 + 4 * i + u, u % RING, n0 // RING + i + u // RING

        def ahead(n):
            return n[0] + RING, n[1], n[2] + 1

        def split_act(act, n):
            num, slot, turn = n
            act.wait_ge(staged[slot], (turn + 1) * 16)
            if not (isinstance(num, int) and num < RING):
                act.wait_ge(unit_used, num - (RING - 1))
            nc.scalar.activation(wH[:, slot, :], stage[:, slot, :], ACT.Copy, scale=WSCALE).then_inc(hi_ready, 1)

        def split_dve(dve, n):
            num, slot, turn = n
            dve.wait_ge(hi_ready, num + 1)
            nc.vector.scalar_tensor_tensor(out=wL[:, slot, :], in0=stage[:, slot, :], scalar=WSCALE,
                                           in1=wH[:, slot, :], op0=ALU.mult,
                                           op1=ALU.subtract).then_inc(lo_ready, 1)

        THREE = [(0, 0), (0, 1), (1, 0)]

        def fm_unit(pe, n, ks, xs, out, first, last, k_wait=None):
            num, slot, _ = n
            pe.wait_ge(lo_ready, num + 1)
            w = (wH, wL)
            for j, k in enumerate(ks):
                if k_wait is not None:
                    k_wait(k)
                for a, b in THREE:
                    for hf in range(2):
                        m = nc.tensor.matmul(out[:, hf, :], w[a][:, slot, 128 * j:128 * (j + 1)],
                                             xs[b][:, k, HALF * hf:HALF * (hf + 1)],
                                             start=(first and j == 0 and (a, b) == THREE[0]),
                                             stop=(last and j == len(ks) - 1 and (a, b) == THREE[2]))
            m.then_inc(unit_used, 1)

        def pe_fm_seg(pe, name, ready, bank_wait=None):
            with pe.Fori(0, 2) as i:
                for u in range(4):
                    if bank_wait is not None:
                        bank_wait(u)
                    pe.wait_ge(free[name], 4 * i + u + 1)
                    fm_unit(pe, unit(name, i, u), range(KD), (hnH, hnL), pair(u), True, True,
                            k_wait=ready if u == 0 else None)

        def pe_tm_seg(pe, name, chunks, ready=None):
            with pe.Fori(0, chunks) as c:
                for u in range(4):
                    num, slot, _ = unit(name, c, u)
                    pe.wait_ge(lo_ready, num + 1)
                    for tt in range(TT):
                        if u == 0:
                            pe.wait_ge(free[name], TT * c + tt + 1)
                        rows = ROWS[tt]
                        for kk in range(2):
                            if ready is not None and tt == 0:
                                ready(2 * u + kk)
                            for a, b in THREE:
                                m = nc.tensor.matmul(
                                    PS[0:rows, tt, :], (hnH, hnL)[b][:, 2 * u + kk, 128 * tt:128 * tt + rows],
                                    (wH, wL)[a][:, slot, 512 * kk:512 * (kk + 1)],
                                    start=(u == 0 and kk == 0 and (a, b) == THREE[0]),
                                    stop=(u == 3 and kk == 1 and (a, b) == THREE[2]))
                        if tt == TT - 1:
                            m.then_inc(unit_used, 1)
                        elif u == 3:
                            m.then_inc(tile_done[name], 1)

        def tm_done(eng, name, c, tt):
            if tt < TT - 1:
                eng.wait_ge(tile_done[name], (TT - 1) * c + tt + 1)
            else:
                eng.wait_ge(unit_used, SEG0[name] + 4 * c + 4)

        def pe_norm(pe, i, summed, count):
            pe.wait_ge(summed, count)
            for hf in range(2):
                m = nc.tensor.matmul(PS[:, 6 + hf, 0:HALF], ones, sqsum[:, HALF * hf:HALF * (hf + 1)],
                                     start=True, stop=True)
            m.then_inc(nrm[i]["ps"], 1)

        def act_norm(act, i):
            act.preload_act_table_set("natural_log_exp_and_others")
            act.wait_ge(nrm[i]["ps"], 1)
            link("A", act, nc.scalar.activation(halves(rstd[:, :]), pair(3), ACT.Ln, bias=eps, scale=1.0 / D))
            nc.scalar.activation(rstd[:, :], rstd[:, :], ACT.Exp, scale=-0.5).then_inc(nrm[i]["rs"], 1)
            for k in range(KD):
                act.wait_ge(nrm[i]["tmp"], k + 1)
                nc.scalar.activation(hnH[:, k, :], ntmp[:, k % 2, :], ACT.Copy).then_inc(nrm[i]["hi"], 1)

        def dve_norm(dve, i, row):
            dve.wait_ge(nrm[i]["rs"], 1)

            def low(k):
                dve.wait_ge(nrm[i]["hi"], k + 1)
                nc.vector.tensor_tensor(hnL[:, k, :], ntmp[:, k % 2, :], hnH[:, k, :],
                                        ALU.subtract).then_inc(nrm[i]["lo"], 1)
            for k in range(KD):
                if k >= 2:
                    dve.wait_ge(nrm[i]["lo"], k - 1)
                nc.vector.scalar_tensor_tensor(out=ntmp[:, k % 2, :], in0=xT[:, k, :], scalar=pd[:, k, row:row + 1],
                                               in1=rstd[:, :], op0=ALU.mult,
                                               op1=ALU.mult).then_inc(nrm[i]["tmp"], 1)
                if k:
                    low(k - 1)
            low(KD - 1)

        def residual(dve, name, m, p, last=False):
            sx, ss = res[name]
            nc.vector.scalar_tensor_tensor(out=halves(xT[:, m, :]), in0=pair(p), scalar=1.0 / WSCALE,
                                           in1=halves(xT[:, m, :]), op0=ALU.mult, op1=ALU.add).then_inc(sx, 1)
            dve.wait_ge(sx, m + 1)
            nc.vector.tensor_tensor(sq[:, :], xT[:, m, :], xT[:, m, :], ALU.mult).then_inc(free[name], 1)
            dve.wait_ge(free[name], m + 1 + (4 if name in ("mout", "sout") else 2))
            nc.vector.tensor_tensor(sqsum[:, :], sqsum[:, :], sq[:, :], ALU.add).then_inc(ss, 1)
            dve.wait_ge(ss, m + 1)

        def dve_fm_res(dve, name):
            link("V", dve, nc.vector.memset(sqsum[:, :], 0.0))
            with dve.Fori(0, 2) as it:
                for u in range(4):
                    n = unit(name, it, u)
                    dve.wait_ge(unit_used, n[0] + 1)
                    residual(dve, name, 4 * it + u, u)
                    split_dve(dve, ahead(n))

        def act_splits(act, name, iters):
            with act.Fori(0, iters) as it:
                for u in range(4):
                    split_act(act, ahead(unit(name, it, u)))

        def pe_ffn(pe, L):
            up, down, f = f"up{L}", f"down{L}", ff[L]
            with pe.Fori(0, KF // 2) as i:
                for s in range(2):
                    pe.wait_ge(f["gate"], 2 * i + s + 1)
                    fm_unit(pe, unit(up, i, 2 * s), range(KD), (hnH, hnL), pair(2 * s), True, True,
                            k_wait=(lambda k: pe.wait_ge(nrm[2 * L + 1]["lo"], k + 1)) if s == 0 else None)
                    pe.wait_ge(f["h32"], 2 * i + s + 1)
                    fm_unit(pe, unit(up, i, 2 * s + 1), range(KD), (hnH, hnL), pair(2 * s + 1), True, True)
            pe.wait_ge(f["h32"], 2 + KF - 1)

            def two(i, name=down):
                for s in range(2):
                    pe.wait_ge(free[name], 2 * i + s + 1)
                    k0 = 0
                    for u in range(4):
                        n = SEG0[name] + 8 * i + 4 * s + u, u, None
                        fm_unit(pe, n, range(k0, k0 + DOWN_K[u]), (hH, hL), pair(s), u == 0, u == 3,
                                k_wait=(lambda k: pe.wait_ge(f["hL"], k + 3)) if s == 0 else None)
                        k0 += DOWN_K[u]
            with pe.Fori(0, 3) as i:
                two(i)
            if L == 1:
                for g in range(2 * KF // 4):
                    if g >= 4:
                        pe.wait_ge(cin, g - 3)
                    pe.wait_ge(f["tail"], KF)
                    for q in range(4):
                        lay, t = divmod(4 * g + q, KF)
                        m = nc.tensor.transpose(PS[0:NCO, 4 + g % 4, 128 * q:128 * (q + 1)],
                                                convO[:, lay, t, :], ident)
                    m.then_inc(ctr, 1)
            two(3)

        def act_ffn(act, L):
            up, down, f = f"up{L}", f"down{L}", ff[L]
            act.preload_act_table(ACT.Gelu)
            with act.Fori(0, KF // 2) as i:
                for s in range(2):
                    t = 2 * i + s
                    ng, nu = unit(up, i, 2 * s), unit(up, i, 2 * s + 1)
                    act.wait_ge(f["hist"], t + 1)
                    act.wait_ge(unit_used, ng[0] + 1)
                    ps = pair(2 * s)
                    nc.scalar.activation(G[:, s, 2:2 + HALF], ps[:, 0, :], ACT.Copy, scale=1.0 / WSCALE)
                    nc.scalar.activation(G[:, s, 2 + HALF:2 + SEQ], ps[:, 1, 0:SEQ - HALF], ACT.Copy,
                                         scale=1.0 / WSCALE)
                    nc.scalar.activation(
                        G[:, s, 2 + SEQ:GC].rearrange("p (b c) -> p b c", c=2 + TB)[:, :, 2:2 + TB],
                        ps[:, 1, SEQ - HALF:HALF].rearrange("p (b c) -> p b c", c=TB), ACT.Copy,
                        scale=1.0 / WSCALE).then_inc(f["gate"], 1)
                    act.wait_ge(f["gate"], t + 3)
                    nc.scalar.activation(acc[:, s, 0:CC], G[:, s, 2:GC], ACT.Identity, bias=pff[:, t, 38 + L:39 + L],
                                         scale=pff[:, t, 32 + 3 * L + 2:33 + 3 * L + 2]).then_inc(f["acc"], 1)
                    split_act(act, ahead(ng))
                    act.wait_ge(f["conv"], t + 3)
                    nc.scalar.activation(acc[:, s, 0:CC], acc[:, s, 0:CC], ACT.Gelu).then_inc(f["gelu"], 1)
                    split_act(act, ahead(nu))
                    act.wait_ge(f["h32"], t + 3)
                    nc.scalar.activation(hH[:, t, :], h32[:, s, :], ACT.Copy).then_inc(f["hH"], 1)
            with act.Fori(0, 3) as i:
                for u in range(8):
                    split_act(act, (SEG0[down] + 8 * i + u + RING, u % 4, (SEG0[down] + u) // 4 + 2 * i + 1))
            if L == 1:
                for g in range(2 * KF // 4):
                    act.wait_ge(ctr, g + 1)
                    nc.scalar.activation(crow[:, :, :].rearrange("p a b -> p (a b)")[:, 512 * g:512 * (g + 1)],
                                         PS[0:NCO, 4 + g % 4, :], ACT.Copy).then_inc(cin, 1)
                for u in range(4):
                    split_act(act, (SEG0[down] + 24 + u + RING, u, (SEG0[down] + 24) // 4 + 1))
            else:
                for u in range(8):
                    split_act(act, (SEG0[down] + 24 + u + RING, u % 4, (SEG0[down] + 24 + u) // 4 + 1))

        def dve_ffn(dve, L):
            up, down, f = f"up{L}", f"down{L}", ff[L]
            with dve.Fori(0, KF // 2) as i:
                for s in range(2):
                    t = 2 * i + s
                    ng, nu = unit(up, i, 2 * s), unit(up, i, 2 * s + 1)
                    dve.wait_ge(f["acc"], t + 1)
                    nc.vector.scalar_tensor_tensor(
                        out=acc[:, s, 0:CC], in0=G[:, s, 0:CC], scalar=pff[:, t, 32 + 3 * L:33 + 3 * L],
                        in1=acc[:, s, 0:CC], op0=ALU.mult, op1=ALU.add).then_inc(f["half"], 1)
                    dve.wait_ge(f["half"], t + 1)
                    nc.vector.scalar_tensor_tensor(
                        out=acc[:, s, 0:CC], in0=G[:, s, 1:1 + CC], scalar=pff[:, t, 33 + 3 * L:34 + 3 * L],
                        in1=acc[:, s, 0:CC], op0=ALU.mult, op1=ALU.add).then_inc(f["conv"], 1)
                    split_dve(dve, ahead(ng))
                    dve.wait_ge(unit_used, nu[0] + 1)
                    dve.wait_ge(f["gelu"], t + 1)
                    dve.wait_ge(f["hL"], t + 1)
                    ps = pair(2 * s + 1)
                    for out, a, b in (
                            (h32[:, s, 0:HALF], ps[:, 0, :], acc[:, s, 0:HALF]),
                            (h32[:, s, HALF:SEQ], ps[:, 1, 0:SEQ - HALF], acc[:, s, HALF:SEQ]),
                            (h32[:, s, SEQ:T].rearrange("p (b c) -> p b c", c=TB),
                             ps[:, 1, SEQ - HALF:HALF].rearrange("p (b c) -> p b c", c=TB),
                             acc[:, s, 2 + SEQ:GC].rearrange("p (b c) -> p b c", c=2 + TB)[:, :, 0:TB])):
                        last = nc.vector.scalar_tensor_tensor(out=out, in0=a, scalar=1.0 / WSCALE, in1=b,
                                                              op0=ALU.mult, op1=ALU.mult)
                    last.then_inc(f["h32"], 1)
                    split_dve(dve, ahead(nu))
                    dve.wait_ge(f["hH"], t + 1)
                    nc.vector.tensor_tensor(hL[:, t, :], h32[:, s, :], hH[:, t, :],
                                            ALU.subtract).then_inc(f["hL"], 1)
            link("V", dve, nc.vector.memset(sqsum[:, :], 0.0))

            def two(i, last):
                for s in range(2):
                    for u in range(4):
                        if last and s == 1:
                            break
                        v = 4 * s + u
                        split_dve(dve, (SEG0[down] + 8 * i + v + RING, u, None))
                    dve.wait_ge(unit_used, SEG0[down] + 8 * i + 4 * s + 4)
                    residual(dve, down, 2 * i + s, s)
            with dve.Fori(0, 3) as i:
                two(i, False)
            two(3, L == 1)

        def pool_ffn(pool, L):
            f = ff[L]
            nc.gpsimd.memset(G[:, :, 0:2], 0.0).then_inc(pads, 1)
            pool.wait_ge(pads, L + 1)
            with pool.Fori(0, KF // 2) as i:
                for s in range(2):
                    t = 2 * i + s
                    pool.wait_ge(f["conv"], t + 1)
                    nc.gpsimd.tensor_copy(
                        G[:, s, 2 + SEQ:GC].rearrange("p (b c) -> p b c", c=2 + TB)[:, :, 0:2],
                        pff[:, t, 16 * L:16 * L + 16].rearrange("p (b c) -> p b c", c=2)).then_inc(f["hist"], 1)
                    pool.wait_ge(f["gate"], t + 3)
                    nc.gpsimd.tensor_copy(convO[:, L, t, 0:2], G[:, s, SEQ:SEQ + 2])
                    nc.gpsimd.tensor_copy(
                        convO[:, L, t, 2:NCO].rearrange("p (b c) -> p b c", c=2),
                        G[:, s, 2 + SEQ:GC].rearrange("p (b c) -> p b c", c=2 + TB)[:, :, TB:TB + 2]) \
                        .then_inc(f["tail"], 1)
                    pool.wait_ge(f["tail"], t + 1)

        TRANSPOSES = [("cache", i) for i in range(4)] + [("q", (c, tt)) for c in range(2) for tt in range(TT)] \
            + [("k", tt) for tt in range(TT)]
        NTR = len(TRANSPOSES)
        ITEMS = [(n, j) for n in range(4) for j in range(KVH)] + [(-1, b) for b in range(NB)]
        NI = len(ITEMS)
        ACT_PT = [sum(n != 0 for n, _ in ITEMS[:x + 1]) for x in range(NI)]
        DVE_PT = [sum(n >= 0 for n, _ in ITEMS[:x + 1]) for x in range(NI)]

        def tr_evac(eng, copy, g, s):
            kind, args = TRANSPOSES[g]
            eng.wait_ge(asem["tr"], g + 1)
            ps = PS[:, g % 8, :].rearrange("p (q t) -> p q t", q=4)
            if kind == "cache":
                J, b = divmod(4 * args, NB)
                m = copy(KcT[:, J, b:b + 4, :], ps)
            elif kind == "q":
                c, tt = args
                if tt < 4:
                    m = copy(qTT[:, c, :, 128 * tt:128 * (tt + 1)], ps)
                else:
                    m = copy(qS[:, c, :, :].rearrange("p b (g t) -> p g b t", t=TB),
                             ps[:, :, 0:NS].rearrange("p g (b t) -> p g b t", t=TB))
            else:
                m = copy(kTT[:, :, 128 * args:128 * args + ROWS[args]], ps[:, 0:2, 0:ROWS[args]])
            m.then_inc(s, 1)

        def out_of(x):
            n, j = ITEMS[x]
            if n >= 0:
                return (PS[:, 6 + x % 2, 0:256].rearrange("p (a q) -> p a q", a=2),
                        slice(128 * n, 128 * (n + 1)), slice(2 * j, 2 * j + 2))
            return (PS[:, 6 + x % 2, 0:64].rearrange("p (a q) -> p a q", a=KD),
                    slice(SEQ + TB * j, SEQ + TB * (j + 1)), slice(0, KD))

        @block.tensor
        def _(pe):
            pe.wait_ge(dC, 32)
            pe.wait_ge(dX, 16 * TT)
            for tt in range(TT):
                if tt == 4:
                    pe.wait_ge(xA, 1)
                r = ROWS[tt]
                for k in range(KD):
                    m = nc.tensor.transpose(PS[:, 2 * (tt % 4) + k // 4, 128 * (k % 4):128 * (k % 4) + r],
                                            xtok[0:r, tt, 128 * k:128 * (k + 1)], ident[0:r, 0:r])
                m.then_inc(x_tr, 1)
            pe.wait_ge(dRows, 16 * 5)
            pe.wait_ge(xV, 1)
            pe.wait_ge(xA, 2)
            for k in range(KD):
                nc.tensor.transpose(PS[:, 4, 5 * k:5 * (k + 1)], rowsD[:, 128 * k:128 * (k + 1)], ident[0:5, 0:5])
            for k in range(KF):
                m = nc.tensor.transpose(PS[:, 2 + k // 12, 40 * (k % 12):40 * (k % 12) + 40],
                                        rowsF[:, 128 * k:128 * (k + 1)], ident[0:40, 0:40])
            m.then_inc(par_tr, 1)

            pe_norm(pe, 0, sq_in, KD + 1)
            pe.wait_ge(gsem["w_lo"], 1)
            pe.wait_ge(nrm[0]["rs"], 1)
            for k in range(KD):
                pe.wait_ge(nrm[0]["lo"], k + 1)
                for a, b in THREE:
                    for hf in range(2):
                        m = nc.tensor.matmul(PS[0:64, 6 + hf, 0:HALF], (gwH, gwL)[a][:, k, :],
                                             (hnH, hnL)[b][:, k, HALF * hf:HALF * (hf + 1)],
                                             start=(k == 0 and (a, b) == THREE[0]),
                                             stop=(k == KD - 1 and (a, b) == THREE[2]))
            m.then_inc(gsem["ps"], 1)
            pe.wait_ge(par_in, 2)
            pe_fm_seg(pe, "qk", None, lambda u: pe.wait_ge(gsem["in"], 2) if u == 3 else None)
            pe.wait_ge(free["qk"], 4 + 7)
            pe_tm_seg(pe, "v", 2)
            pe.wait_ge(gsem["rows"], 1)
            pe.wait_ge(dMisc, 16 * 3)
            for tt in range(TT):
                r = ROWS[tt]
                for j, row in enumerate((LI, WS)):
                    nc.tensor.transpose(PS[0:r, 5, 8 * tt + 4 * j:8 * tt + 4 * j + 4],
                                        row[:, 128 * tt:128 * tt + r], ident[0:4, 0:4])
            nc.tensor.transpose(PS[:, 5, 64:96], n0r[:, :], ident[0:32, 0:32]).then_inc(gsem["tr"], 1)
            pe.wait_ge(free["qk"], 4 + 8)
            for tt in range(TT):
                if tt >= 2:
                    pe.wait_ge(gsem["kw"], tt - 1)
                r = ROWS[tt]
                for h in range(MH):
                    m = nc.tensor.transpose(PS[0:r, 6 + tt % 2, 128 * h:128 * (h + 1)],
                                            kT[:, h, 128 * tt:128 * tt + r], ident)
                m.then_inc(gsem["kt"], 1)
            pe.wait_ge(free["v"], TT + 9)

            def o_banks(u):
                if u == 2:
                    pe.wait_ge(free["v"], TT + 10)
                    pe.wait_ge(gsem["cols"], 1)
                if u == 3:
                    pe.wait_ge(gsem["kts"], 1)
            pe_fm_seg(pe, "o", None, o_banks)

            wcol = [0, 512, 896, 1152]

            def head_scores(h):
                if h == 0:
                    pe.wait_ge(free["o"], 4 + 8)
                sel = const("sel", 4)[:, 128 * h:128 * (h + 1)]
                nc.tensor.matmul(PS[:, 0, :], sel, R[:, 0:SEQ], start=True, stop=True)
                nc.tensor.matmul(PS[:, 7, 0:3 * NS], sel, R[:, 2 * SEQ:], start=True, stop=True)
                for j, (bank, c0) in enumerate(((2, 0), (3, 0), (7, 192), (3, 384))):
                    n = SEQ - 128 * j
                    nc.tensor.matmul(PS[:, bank, c0:c0 + n], kT[:, h, 128 * j:128 * (j + 1)],
                                     qT[:, h, 128 * j:SEQ], start=True, stop=True)
                nc.tensor.matmul(PS[0:NS, 7, 448:512], kT[:, h, SEQ:T], qT[:, h, SEQ:T],
                                 start=True, stop=True).then_inc(hsem["s"], 1)
                if h:
                    pe.wait_ge(hsem["hs"], h)
                nc.tensor.matmul(PS[:, 1, :], sel, R[:, SEQ:2 * SEQ], start=True, stop=True).then_inc(hsem["e1"], 1)

            def head_sums(h):
                pe.wait_ge(hsem["w"], h + 1)
                if h:
                    pe.wait_ge(hsem["csi"], 2 * h)
                for bank in (4, 5, 6):
                    for j in range(4):
                        lhs = ones if bank == 6 else vM[:, j, 256 * h + 128 * (bank - 4):][:, 0:128]
                        nc.tensor.matmul(PS[:, bank, 128 * j:SEQ], lhs, wbuf[:, wcol[j]:wcol[j] + SEQ - 128 * j],
                                         start=(j == 0), stop=(j == 3), skip_group_check=True)
                pe.wait_ge(dC0[h % 2], 16 * (h // 2 + 1))
                pe.wait_ge(hsem["e1b"], h + 1)
                for e in range(2):
                    nc.tensor.matmul(PS[:, 1, NS * e:NS * (e + 1)], vM[0:NS, 4, 256 * h + 128 * e:][:, 0:128],
                                     wbuf[0:NS, 1280:1280 + NS], start=True, stop=False, skip_group_check=True)
                    for b in range(NB):
                        nc.tensor.matmul(PS[:, 1, NS * e + TB * b:NS * e + TB * (b + 1)],
                                         C0[:, h % 2, b, 128 * e:128 * (e + 1)], qs[:, TB * b:TB * (b + 1)],
                                         start=False, stop=(b == NB - 1), skip_group_check=True)
                nc.tensor.matmul(PS[:, 1, 2 * NS:3 * NS], ones[0:NS, :], wbuf[0:NS, 1280:1280 + NS],
                                 start=True, stop=False, skip_group_check=True)
                nc.tensor.matmul(PS[:, 1, 2 * NS:3 * NS], ones, nqp[:, :], start=False, stop=True,
                                 skip_group_check=True).then_inc(hsem["num"], 1)

            def head_norm(h):
                pe.wait_ge(hsem["sq"], 2 * h + 2)
                for hf in range(2):
                    for e in range(2):
                        m = nc.tensor.matmul(PS[:, 4 + hf, 0:HALF], ones, ntmp[:, e, HALF * hf:HALF * (hf + 1)],
                                             start=(e == 0), stop=(e == 1))
                m.then_inc(hsem["ss"], 1)

            def head_memory(h):
                for j in range(4):
                    nc.tensor.matmul(PS[:, 6, 0:DV], kw[:, j, 128 * h:128 * (h + 1)],
                                     vM[:, j, 256 * h:256 * (h + 1)], start=(j == 0), stop=(j == 3))
                for j in range(4):
                    nc.tensor.matmul(PS[:, 6, 256:257], kw[:, j, 128 * h:128 * (h + 1)], ones[:, 0:1],
                                     start=(j == 0), stop=(j == 3))
                pe.wait_ge(hsem["kwm"], h + 1)
                nc.tensor.matmul(PS[:, 6, 257:257 + NB], kts[:, 128 * h:128 * (h + 1)], wsm[:, :],
                                 start=True, stop=True).then_inc(hsem["cp"], 1)
                if h + 1 < MH:
                    pe.wait_ge(hsem["e1b"], h + 2)
                pe.wait_ge(hsem["rs"], h + 1)
                for rnd, banks in enumerate(((1, 4), (5, 6))):
                    if rnd == 1:
                        pe.wait_ge(hsem["cpi"], h + 1)
                    for i in range(2):
                        for g in range(2):
                            b = 4 * g + 2 * rnd + i
                            m = nc.tensor.matmul(PS[:, banks[g], 256 * i:256 * (i + 1)],
                                                 kwm[32 * g:32 * (g + 1), b, :],
                                                 vM[32 * g:32 * (g + 1), 4, 256 * h:256 * (h + 1)],
                                                 start=True, stop=True)
                    m.then_inc(hsem["cs"], 1)

            head_scores(0)
            for h in range(MH):
                head_sums(h)
                if h + 1 < MH:
                    head_scores(h + 1)
                head_norm(h)
                head_memory(h)
            pe.wait_ge(hsem["csi"], 2 * MH)
            nc.tensor.transpose(PS[0:36, 7, 0:DK], nnew[:, :], ident).then_inc(hsem["ntr"], 1)
            pe_fm_seg(pe, "mout", lambda k: pe.wait_ge(hsem["lo"], k + 1),
                      lambda u: pe.wait_ge(hsem["nin"], 1) if u == 3 else None)
            pe_norm(pe, 1, res["mout"][1], KD)
            pe.wait_ge(nrm[1]["rs"], 1)
            pe_ffn(pe, 0)

            pe_norm(pe, 2, res["down0"][1], KD)
            pe_tm_seg(pe, "qkv", 3, lambda k: pe.wait_ge(nrm[2]["lo"], k + 1))
            pe.wait_ge(nrm[2]["rs"], 1)
            pe.wait_ge(free["qkv"], TT * 4)
            pe.wait_ge(dKV, 16 * 5)
            for g, (kind, args) in enumerate(TRANSPOSES):
                if g >= 8:
                    pe.wait_ge(asem["trA" if g % 2 == 0 else "trV"], (g - 8) // 2 + 1)
                if kind == "cache":
                    for q in range(4):
                        J, b = divmod(4 * args + q, NB)
                        m = nc.tensor.transpose(PS[:, g % 8, 128 * q:128 * (q + 1)],
                                                Kc[:, b, 128 * J:128 * (J + 1)], ident)
                elif kind == "q":
                    c, tt = args
                    pe.wait_ge(asem["rope"], c + 1)
                    r = ROWS[tt]
                    for q in range(4):
                        m = nc.tensor.transpose(
                            PS[:, g % 8, 128 * q:128 * q + r],
                            qtok[0:r, tt, 512 * c + 128 * q:512 * c + 128 * (q + 1)],
                            ident[0:r, 0:r])
                else:
                    tt = args
                    pe.wait_ge(asem["rope"], 3)
                    r = ROWS[tt]
                    for J in range(2):
                        m = nc.tensor.transpose(PS[:, g % 8, 128 * J:128 * J + r],
                                                qtok[0:r, tt, 1024 + 128 * J:1024 + 128 * (J + 1)],
                                                ident[0:r, 0:r])
                m.then_inc(asem["tr"], 1)
            pe.wait_ge(asem["trA"], (NTR + 1) // 2)
            pe.wait_ge(asem["trV"], NTR // 2)

            def scores(x):
                if x >= 2:
                    pe.wait_ge(asem["e"], x - 1)
                n, j = ITEMS[x]
                b0 = 2 * (x % 2)
                if n >= 0:
                    J, p = divmod(j, 2)
                    lo = 0 if n else 128
                    for hp in range(2):
                        o = PS[:, b0 + hp, :].rearrange("p (g k) -> p g k", g=2)
                        nc.tensor.matmul(o[:, :, lo:256], ident16[:, :],
                                         mask16[:, lo:256].unsqueeze(1).to_broadcast([128, 2, 256 - lo]),
                                         start=True, stop=False, skip_group_check=True)
                        for g in range(2):
                            m = nc.tensor.matmul(o[:, g, lo:256],
                                                 qTT[64 * p:64 * p + 64, J, 2 * hp + g, 128 * n:128 * (n + 1)],
                                                 kTT[64 * p:64 * p + 64, J, 128 * (n - 1) + lo:128 * (n + 1)],
                                                 start=False, stop=(g == 1), skip_group_check=True)
                else:
                    b = j
                    nc.tensor.matmul(PS[:, b0, 0:KEYS], ident16[:, :],
                                     mask16[:, 256 + KEYS * b:256 + KEYS * (b + 1)], start=True, stop=False,
                                     skip_group_check=True)
                    for kv in range(KVH):
                        J, p = divmod(kv, 2)
                        q = qS[64 * p:64 * p + 64, J, b, :]
                        nc.tensor.matmul(PS[32 * kv:32 * kv + 32, b0, 0:WIN], q, KcT[64 * p:64 * p + 64, J, b, :],
                                         start=False, stop=False, skip_group_check=True)
                        m = nc.tensor.matmul(PS[32 * kv:32 * kv + 32, b0, WIN:KEYS], q,
                                             kTT[64 * p:64 * p + 64, J, SEQ:T], start=False, stop=True,
                                             skip_group_check=True)
                m.then_inc(asem["s"], 1)

            def turn(x):
                n, j = ITEMS[x]
                pe.wait_ge(asem["p"], x + 1)
                if x:
                    if ACT_PT[x - 1]:
                        pe.wait_ge(asem["ptA"], ACT_PT[x - 1])
                    pe.wait_ge(asem["ptV"], DVE_PT[x - 1])
                if n >= 0:
                    for kb in ((0, 1) if n else (1,)):
                        for g in range(4):
                            m = nc.tensor.transpose(PS[:, 4 + kb, 128 * g:128 * (g + 1)],
                                                    P[:, x % 2, 256 * g + 128 * kb:256 * g + 128 * (kb + 1)], ident)
                else:
                    nc.tensor.transpose(PS[:, 4, 0:128], P[:, x % 2, 0:128], ident)
                    m = nc.tensor.transpose(PS[0:NS, 4, 128:256], P[:, x % 2, 128:KEYS], ident)
                m.then_inc(asem["t"], 1)

            def values(x):
                n, j = ITEMS[x]
                kbs = (0, 1) if n else (1,)
                if ACT_PT[x]:
                    pe.wait_ge(asem["ptA"], ACT_PT[x])
                pe.wait_ge(asem["ptV"], DVE_PT[x])
                if x >= 2:
                    pe.wait_ge(asem["ol"], x - 1)
                ob = 6 + x % 2
                if n >= 0:
                    for r in range(2):
                        for kb in kbs:
                            m = nc.tensor.matmul(
                                PS[64 * r:64 * r + 64, ob, 0:256],
                                qtok[:, n - 1 + kb, 1280 + 64 * j:1280 + 64 * (j + 1)],
                                PT[:, kb, :].rearrange("p (a r q) -> p r a q", r=2, q=128)[:, r],
                                start=(kb == kbs[0]), stop=(kb == 1), skip_group_check=True)
                else:
                    b = j
                    for kv in range(KVH):
                        for r in range(2):
                            o = PS[64 * r:64 * r + 64, ob, 16 * kv:16 * (kv + 1)]
                            cols = slice(32 * kv, 32 * (kv + 1))

                            def mov(a):
                                return a.rearrange("p (a r t) -> p r a t", r=2, t=TB)[:, r]
                            nc.tensor.matmul(o, Vc[:, b, 64 * kv:64 * (kv + 1)], mov(PT[:, 0, cols]),
                                             start=True, stop=False, skip_group_check=True)
                            m = nc.tensor.matmul(o, qtok[0:NS, 4, 1280 + 64 * kv:1280 + 64 * (kv + 1)],
                                                 mov(PT[0:NS, 0, 128 + 32 * kv:128 + 32 * (kv + 1)]),
                                                 start=False, stop=True, skip_group_check=True)
                m.then_inc(asem["o"], 1)

            scores(0)
            scores(1)
            for x in range(NI):
                turn(x)
                if x + 2 < NI:
                    scores(x + 2)
                values(x)
            pe.wait_ge(asem["ol"], NI)
            pe_fm_seg(pe, "sout", None)
            pe_norm(pe, 3, res["sout"][1], KD)
            pe.wait_ge(nrm[3]["rs"], 1)
            pe_ffn(pe, 1)

            pe.wait_ge(res["down1"][0], KD)
            pe.wait_ge(cin, 2 * KF // 4)
            for tt in range(TT):
                if tt == 4:
                    pe.wait_ge(yA, 1)
                r = ROWS[tt]
                for k in range(KD):
                    m = nc.tensor.transpose(PS[0:r, 2 * (tt % 4) + k // 4, 128 * (k % 4):128 * (k % 4 + 1)],
                                            xT[:, k, 128 * tt:128 * tt + r], ident)
                m.then_inc(ytr, 1)

        @block.scalar
        def _(act):
            for s in ("qk", "o"):
                act.sem_inc(free[s], 4)
            act.sem_inc(free["qkv"], TT)
            for L in range(2):
                act.sem_inc(ff[L]["gate"], 2)
            for tt in (0, 2, 4):
                act.wait_ge(x_tr, tt + 1)
                r = ROWS[tt]
                nc.scalar.activation(xT[:, :, 128 * tt:128 * tt + r],
                                     PS[:, 2 * (tt % 4):2 * (tt % 4) + 2, :].rearrange("p a (k t) -> p (a k) t", t=128)
                                     [:, :, 0:r], ACT.Copy).then_inc(xA, 1)
            act.wait_ge(xA, 3)
            act.wait_ge(xV, 2)
            for k in range(KD):
                nc.scalar.activation(sq8[:, k, :], xT[:, k, :], ACT.Square).then_inc(sq_in, 1)
            act.wait_ge(par_tr, 1)
            nc.scalar.activation(pd[:, :, :].rearrange("p k r -> p (k r)"), PS[:, 4, 0:5 * KD], ACT.Copy) \
                .then_inc(par_in, 1)
            nc.scalar.activation(pff[:, 0:12, :].rearrange("p k r -> p (k r)"), PS[:, 2, 0:480], ACT.Copy)
            nc.scalar.activation(pff[:, 12:KF, :].rearrange("p k r -> p (k r)"), PS[:, 3, 0:400], ACT.Copy) \
                .then_inc(par_in, 1)
            for u in range(RING):
                split_act(act, (u, u, 0))
            act.wait_ge(dGate, 16 * 3)
            act.wait_ge(gsem["w_hi"], 1)
            nc.scalar.activation(gwH[:, :, :], gwS[:, :, :], ACT.Copy, scale=WSCALE).then_inc(gsem["w_hi"], 1)
            act_norm(act, 0)

            act.wait_ge(gsem["ps"], 1)
            act.wait_ge(dMisc, 16 * 3)
            nc.scalar.activation(halves(LI[:, :]), PS[0:4, 6:8, 0:HALF], ACT.Identity, bias=gb[:, 0:1],
                                 scale=1.0 / WSCALE).then_inc(gsem["in"], 1)
            nc.scalar.activation(halves(FG[:, :]), PS[32:36, 6:8, 0:HALF], ACT.Identity, bias=gb[:, 1:2],
                                 scale=1.0 / WSCALE).then_inc(gsem["in"], 1)
            act.wait_ge(gsem["in"], 2)
            link("A", act, nc.scalar.activation(GL[:, :], FG[:, :], ACT.Abs))
            link("A", act, nc.scalar.activation(GL[:, :], GL[:, :], ACT.Exp, scale=-1.0))
            nc.scalar.activation(GL[:, :], GL[:, :], ACT.Ln, bias=ones[0:4, 0:1]).then_inc(gsem["softplus"], 1)
            for i, scale in enumerate((1.0 / WSCALE, DK ** -0.5 / WSCALE)):
                for u in range(4):
                    n = unit("qk", i, u)
                    act.wait_ge(unit_used, n[0] + 1)
                    nc.scalar.activation(halves((qT, kT)[i][:, u, :]), pair(u), ACT.Copy, scale=scale) \
                        .then_inc(free["qk"], 1)
                    split_act(act, ahead(n))
            act.wait_ge(gsem["scans"], 1)
            nc.scalar.activation(R[:, SEQ:2 * SEQ], GB[:, 0:SEQ], ACT.Exp, scale=-1.0)
            nc.scalar.activation(R[:, 2 * SEQ + NS:2 * SEQ + 2 * NS], GB[:, SEQ:T], ACT.Exp, scale=-1.0)
            nc.scalar.activation(R[:, 2 * SEQ + 2 * NS:], R[:, 2 * SEQ + 2 * NS:], ACT.Exp)
            nc.scalar.activation(WS[:, 0:SEQ], LI[:, 0:SEQ], ACT.Exp, bias=R[:, SEQ - 1:SEQ])
            nc.scalar.activation(WS[:, SEQ:T], WS[:, SEQ:T], ACT.Exp).then_inc(gsem["rows"], 1)
            act.preload_act_table(ACT.Sigmoid)
            act_splits(act, "v", 2)
            act.wait_ge(gsem["cols"], 1)
            for j in range(4):
                act.wait_ge(gsem["kt"], j + 1)
                for h in range(MH):
                    m = nc.scalar.activation(kw[:, j, 128 * h:128 * (h + 1)], PS[:, 6 + j % 2, 128 * h:128 * (h + 1)],
                                             ACT.Copy, scale=gcol[:, j, 4 + h:5 + h])
                m.then_inc(gsem["kw"], 1)
            act.wait_ge(gsem["kt"], TT)
            nc.scalar.activation(kts[:, :], PS[0:NS, 6, :], ACT.Copy).then_inc(gsem["kts"], 1)
            with act.Fori(0, 2) as i:
                for u in range(4):
                    n = unit("o", i, u)
                    act.wait_ge(unit_used, n[0] + 1)
                    nc.scalar.activation(halves(so[:, 4 * i + u, :]), pair(u), ACT.Sigmoid, scale=1.0 / WSCALE) \
                        .then_inc(free["o"], 1)
                    split_act(act, ahead(n))

            wcol = [0, 512, 896, 1152]
            act.preload_act_table_set("natural_log_exp_and_others")

            def head_exps(h):
                act.wait_ge(hsem["dt"], h + 1)
                for j in range(4):
                    a = gcol[:, j, h:h + 1]
                    nc.scalar.activation(wbuf[:, wcol[j]:wcol[j] + 128], dtmp[:, 128 * j:128 * (j + 1)],
                                         ACT.Exp, bias=a)
                    if j < 3:
                        nc.scalar.activation(wbuf[:, wcol[j] + 128:wcol[j] + SEQ - 128 * j],
                                             PS[:, 0, 128 * (j + 1):SEQ], ACT.Exp, bias=a)
                nc.scalar.activation(wbuf[0:NS, 1280:1280 + NS], dtmp[0:NS, 512:512 + NS], ACT.Exp,
                                     bias=gcol[0:NS, 4, h:h + 1]).then_inc(hsem["e"], 1)
                act.wait_ge(hsem["e1"], h + 1)
                nc.scalar.activation(e1b[:, :], PS[:, 1, :], ACT.Copy).then_inc(hsem["e1b"], 1)

            wcol = [0, 512, 896, 1152]
            act.wait_ge(gsem["m_out"], 32)
            head_exps(0)
            for h in range(MH):
                act.wait_ge(hsem["num"], h + 1)
                nc.scalar.activation(sq[:, 0:SEQ], PS[:, 6, :], ACT.Abs)
                nc.scalar.activation(sq[:, SEQ:T], PS[:, 1, 2 * NS:3 * NS], ACT.Abs).then_inc(hsem["abs"], 1)
                act.wait_ge(hsem["hs"], h + 1)
                nc.scalar.activation(ntmp[:, 0, :], hsA[:, :], ACT.Square).then_inc(hsem["sq"], 1)
                nc.scalar.activation(ntmp[:, 1, :], hsB[:, :], ACT.Square).then_inc(hsem["sq"], 1)
                if h + 1 < MH:
                    head_exps(h + 1)
                act.wait_ge(hsem["ss"], h + 1)
                link("A", act, nc.scalar.activation(halves(rstd[:, :]), PS[:, 4:6, 0:HALF], ACT.Ln, bias=eps,
                                                    scale=1.0 / DV))
                nc.scalar.activation(rstd[:, :], rstd[:, :], ACT.Exp, scale=-0.5).then_inc(hsem["rs"], 1)
                for e, hs in enumerate((hsA, hsB)):
                    act.wait_ge(hsem["f"], 2 * h + e + 1)
                    nc.scalar.activation(hnH[:, 2 * h + e, :], hs[:, :], ACT.Copy).then_inc(hsem["hi"], 1)
            act.wait_ge(hsem["ntr"], 1)
            nc.scalar.activation(nrow[:, :], PS[0:36, 7, 0:DK], ACT.Copy).then_inc(hsem["nin"], 1)
            act_splits(act, "mout", 2)
            act_norm(act, 1)
            act_ffn(act, 0)
            act_norm(act, 2)

            def rms(c):
                act.wait_ge(asem["rss"], c + 1)
                link("A", act, nc.scalar.activation(rss[:, :, :], rss[:, :, :], ACT.Ln, bias=eps, scale=1.0 / HD))
                nc.scalar.activation(rss[:, :, :], rss[:, :, :], ACT.Exp, scale=-0.5).then_inc(asem["rs"], 1)

            act.wait_ge(asem["cz"], 1)
            for c in range(3):
                for u in range(3):
                    split_act(act, ahead(unit("qkv", c, u)))
                    if c and u == 0:
                        rms(c - 1)
                for tt in range(TT):
                    tm_done(act, "qkv", c, tt)
                    src, dst = PS[0:ROWS[tt], tt, :], qtok[0:ROWS[tt], tt, 512 * c:512 * (c + 1)]
                    if c < 2:
                        src = src.rearrange("p (a g d) -> p a g d", a=2, d=HD)
                        dst = dst.rearrange("p (g a d) -> p a g d", a=2, d=HD)
                    nc.scalar.activation(dst, src, ACT.Copy, scale=1.0 / WSCALE).then_inc(free["qkv"], 1)
                split_act(act, ahead(unit("qkv", c, 3)))
            rms(2)
            for g in range(0, NTR, 2):
                tr_evac(act, lambda o, i: nc.scalar.activation(o, i, ACT.Copy), g, asem["trA"])

            def exps(x):
                n, j = ITEMS[x]
                act.wait_ge(asem["m"], x + 1)
                s = st[:, x % 2]
                if n >= 0:
                    lo = 0 if n else 128
                    src = PS[:, 2 * (x % 2):2 * (x % 2) + 2, :].rearrange("p a b -> p (a b)")
                    for g in range(4):
                        nc.scalar.activation(P[:, x % 2, 256 * g + lo:256 * (g + 1)],
                                             src[:, 256 * g + lo:256 * (g + 1)], ACT.Exp, bias=s[:, 2, g:g + 1],
                                             scale=HD ** -0.5, accum_out=s[:, 4, g:g + 1])
                    w = 4
                else:
                    nc.scalar.activation(P[:, x % 2, 0:KEYS], PS[:, 2 * (x % 2), 0:KEYS], ACT.Exp,
                                         bias=s[:, 2, 0:1], scale=HD ** -0.5, accum_out=s[:, 4, 0:1])
                    w = 1
                nc.scalar.activation(s[:, 5, 0:w], s[:, 3, 0:w], ACT.Exp).then_inc(asem["e"], 1)

            def out_high(x):
                act.wait_ge(asem["o"], x + 1)
                src, cols, tiles = out_of(x)
                nc.scalar.activation(hnH[:, tiles, cols], src, ACT.Copy).then_inc(asem["oh"], 1)

            exps(0)
            exps(1)
            for x in range(NI):
                n, j = ITEMS[x]
                act.wait_ge(asem["t"], x + 1)
                if n != 0:
                    if x:
                        act.wait_ge(asem["o"], x)
                    if n > 0:
                        nc.scalar.activation(PT[:, 0, :], PS[:, 4, :], ACT.Copy).then_inc(asem["ptA"], 1)
                    else:
                        nc.scalar.activation(PT[:, 0, 0:128], PS[:, 4, 0:128], ACT.Copy)
                        nc.scalar.activation(PT[0:NS, 0, 128:256], PS[0:NS, 4, 128:256], ACT.Copy) \
                            .then_inc(asem["ptA"], 1)
                if x:
                    out_high(x - 1)
                if x + 2 < NI:
                    exps(x + 2)
            out_high(NI - 1)
            act_splits(act, "sout", 2)
            act_norm(act, 3)
            act_ffn(act, 1)
            for tt in (0, 2, 4):
                act.wait_ge(ytr, tt + 1)
                r = ROWS[tt]
                nc.scalar.activation(ytok[0:r, tt, :].rearrange("p (a b) -> p a b", a=2),
                                     PS[0:r, 2 * (tt % 4):2 * (tt % 4) + 2, :], ACT.Copy).then_inc(yA, 1)

        @block.vector
        def _(dve):
            dve.sem_inc(free["v"], TT)
            dve.sem_inc(free["mout"], 4)
            dve.sem_inc(free["sout"], 4)
            for L in range(2):
                dve.sem_inc(free[f"down{L}"], 2)
                dve.sem_inc(ff[L]["conv"], 2)
                dve.sem_inc(ff[L]["h32"], 2)
                dve.sem_inc(ff[L]["hL"], 2)
            dve.wait_ge(dC, 32)
            nc.vector.tensor_copy(ident16[:, :], ident)
            nc.vector.tensor_copy(mask16[:, :], masks).then_inc(masks_in, 1)
            for tt in (1, 3):
                dve.wait_ge(x_tr, tt + 1)
                nc.vector.tensor_copy(xT[:, :, 128 * tt:128 * tt + 128],
                                      PS[:, 2 * tt:2 * tt + 2, :].rearrange("p a (k t) -> p (a k) t", t=128)) \
                    .then_inc(xV, 1)
            dve.wait_ge(sq_in, KD)
            nc.vector.tensor_reduce(sqsum[:, :], sq8[:, :, :].rearrange("p k t -> p t k"), AX.X, ALU.add) \
                .then_inc(sq_in, 1)
            for u in range(RING):
                split_dve(dve, (u, u, 0))
            dve.wait_ge(gsem["w_hi"], 2)
            nc.vector.scalar_tensor_tensor(out=gwL[:, :, :], in0=gwS[:, :, :], scalar=WSCALE, in1=gwH[:, :, :],
                                           op0=ALU.mult, op1=ALU.subtract).then_inc(gsem["w_lo"], 1)
            dve.wait_ge(par_in, 2)
            dve_norm(dve, 0, 0)

            dve.wait_ge(gsem["softplus"], 1)
            link("V", dve, nc.vector.scalar_tensor_tensor(out=GL[:, :], in0=FG[:, :], scalar=0.0, in1=GL[:, :],
                                                          op0=ALU.min, op1=ALU.subtract))
            link("V", dve, nc.vector.tensor_tensor_scan(GB[:, :], const("keep", 4), GL[:, :], 0.0,
                                                        ALU.mult, ALU.add))
            link("V", dve, nc.vector.tensor_tensor(LI[:, :], LI[:, :], GB[:, :], ALU.subtract))
            link("V", dve, nc.vector.tensor_copy(GA2[:, :], LI[:, :]))
            dve.wait_ge(dMisc, 16 * 3)

            def samples(a):
                return a.rearrange("p (b t) -> p b t", t=TB)
            m0 = m0T[:, :].unsqueeze(2)
            nc.vector.tensor_scalar(GA2[:, 0:1], LI[:, 0:1], 0.0, None, ALU.max)
            link("V", dve, nc.vector.tensor_tensor(samples(GA2[:, SEQ:T])[:, :, 0:1], samples(LI[:, SEQ:T])[:, :, 0:1],
                                                   m0, ALU.max))
            link("V", dve, nc.vector.tensor_tensor_scan(GM[:, :], const("drop", 4), GA2[:, :], 0.0,
                                                        ALU.add, ALU.max))
            nc.vector.tensor_tensor(GB[:, :], GB[:, :], GM[:, :], ALU.add)
            nc.vector.tensor_scalar(R[:, 0:SEQ], GM[:, 0:SEQ], -1.0, None, ALU.mult)
            nc.vector.tensor_scalar(R[:, 2 * SEQ:2 * SEQ + NS], GM[:, SEQ:T], -1.0, None, ALU.mult)
            nc.vector.tensor_tensor(samples(R[:, 2 * SEQ + 2 * NS:]), m0.to_broadcast([4, NB, TB]),
                                    samples(GM[:, SEQ:T]), ALU.subtract)
            nc.vector.tensor_tensor(samples(WS[:, SEQ:T]), samples(LI[:, SEQ:T]),
                                    samples(GM[:, SEQ:T])[:, :, TB - 1:TB].to_broadcast([4, NB, TB]),
                                    ALU.subtract).then_inc(gsem["scans"], 1)
            with dve.Fori(0, 2) as i:
                for u in range(4):
                    split_dve(dve, ahead(unit("qk", i, u)))
            for c in range(2):
                for u in range(3):
                    split_dve(dve, ahead(unit("v", c, u)))
                for tt in range(TT):
                    tm_done(dve, "v", c, tt)
                    nc.vector.tensor_scalar(vM[0:ROWS[tt], tt, 512 * c:512 * (c + 1)], PS[0:ROWS[tt], tt, :],
                                            1.0 / WSCALE, None, ALU.mult).then_inc(free["v"], 1)
                split_dve(dve, ahead(unit("v", c, 3)))
            dve.wait_ge(gsem["tr"], 1)
            nc.vector.tensor_copy(gcol[:, 0:4, :].rearrange("p a b -> p (a b)"), PS[:, 5, 0:32])
            nc.vector.tensor_copy(gcol[0:NS, 4, :], PS[0:NS, 5, 32:40])
            nc.vector.tensor_copy(n0T[:, :], PS[:, 5, 64:96]).then_inc(gsem["cols"], 1)
            dve.wait_ge(gsem["cols"], 1)
            with dve.Fori(0, 2) as i:
                for u in range(4):
                    split_dve(dve, ahead(unit("o", i, u)))

            def head_weights(h):
                dve.wait_ge(hsem["s"], h + 1)
                n0h = n0T[:, :].rearrange("p (b h) -> p b h", h=MH)[:, :, h:h + 1]
                nc.vector.tensor_tensor(dtmp[:, 0:512].rearrange("p (j t) -> p j t", t=128),
                                        PS[:, 0, :].rearrange("p (j t) -> p j t", t=128),
                                        const("cmask").unsqueeze(1).to_broadcast([128, 4, 128]), ALU.add)
                nc.vector.tensor_tensor(dtmp[0:NS, 512:512 + NS], PS[0:NS, 7, 0:NS], const("bmask", NS), ALU.add) \
                    .then_inc(hsem["dt"], 1)
                link("V", dve, nc.vector.tensor_copy(wis[:, :], PS[:, 7, NS:3 * NS]))
                link("V", dve, nc.vector.tensor_tensor(qs[:, :], qT[:, h, SEQ:T], wis[:, NS:2 * NS], ALU.mult))
                nc.vector.tensor_tensor(samples(nqp[:, :]), samples(qs[:, :]), n0h.to_broadcast([128, NB, TB]), ALU.mult)
                dve.wait_ge(hsem["e"], h + 1)
                nc.vector.tensor_tensor(wbuf[:, 0:512], wbuf[:, 0:512], PS[:, 2, :], ALU.mult)
                nc.vector.tensor_tensor(wbuf[:, 512:896], wbuf[:, 512:896], PS[:, 3, 0:384], ALU.mult)
                nc.vector.tensor_tensor(wbuf[:, 896:1152], wbuf[:, 896:1152], PS[:, 7, 192:448], ALU.mult)
                nc.vector.tensor_tensor(wbuf[:, 1152:1280], wbuf[:, 1152:1280], PS[:, 3, 384:512], ALU.mult)
                nc.vector.tensor_tensor(wbuf[0:NS, 1280:1280 + NS], wbuf[0:NS, 1280:1280 + NS],
                                        PS[0:NS, 7, 448:512], ALU.mult).then_inc(hsem["w"], 1)

            def head_keys(h):
                if h:
                    dve.wait_ge(hsem["csi"], 2 * h)
                link("V", dve, nc.vector.tensor_copy(dec[:, :].unsqueeze(2), samples(wis[:, NS:2 * NS])[:, :, TB - 1:TB]))
                link("V", dve, nc.vector.tensor_scalar(wsm[:, :], const("blk", NS), gcol[0:NS, 4, 4 + h:5 + h], None,
                                                       ALU.mult))
                nc.vector.tensor_tensor(kwm[:, :, :], kts[:, 128 * h:128 * (h + 1)].unsqueeze(1).to_broadcast([NS, NB, DK]),
                                        wsm[:, :].unsqueeze(2).to_broadcast([NS, NB, DK]), ALU.mult) \
                    .then_inc(hsem["kwm"], 1)

            dve.wait_ge(gsem["m_out"], 32)
            dve.wait_ge(gsem["kts"], 1)
            head_weights(0)
            for h in range(MH):
                head_keys(h)
                dve.wait_ge(hsem["abs"], h + 1)
                dve.wait_ge(hsem["e1b"], h + 1)
                nc.vector.tensor_tensor(sq[:, 0:SEQ], sq[:, 0:SEQ], e1b[:, :], ALU.max)
                link("V", dve, nc.vector.tensor_tensor(sq[:, SEQ:T], sq[:, SEQ:T], wis[:, 0:NS], ALU.max))
                link("V", dve, nc.vector.reciprocal(rstd[:, :], sq[:, :]))
                for e, hs in enumerate((hsA, hsB)):
                    nc.vector.tensor_tensor(hs[:, 0:SEQ], rstd[:, 0:SEQ], PS[:, 4 + e, :], ALU.mult)
                    m = nc.vector.tensor_tensor(hs[:, SEQ:T], rstd[:, SEQ:T], PS[:, 1, NS * e:NS * (e + 1)], ALU.mult)
                m.then_inc(hsem["hs"], 1)
                dve.wait_ge(hsem["hs"], h + 1)
                if h + 1 < MH:
                    head_weights(h + 1)
                dve.wait_ge(hsem["rs"], h + 1)
                for e, hs in enumerate((hsA, hsB)):
                    link("V", dve, nc.vector.scalar_tensor_tensor(out=hs[:, :], in0=hs[:, :],
                                                                  scalar=pd[:, 2 * h + e, 4:5], in1=rstd[:, :],
                                                                  op0=ALU.mult, op1=ALU.mult))
                    nc.vector.tensor_tensor(hs[:, :], hs[:, :], so[:, 2 * h + e, :], ALU.mult).then_inc(hsem["f"], 1)
                for e, hs in enumerate((hsA, hsB)):
                    dve.wait_ge(hsem["hi"], 2 * h + e + 1)
                    nc.vector.tensor_tensor(hnL[:, 2 * h + e, :], hs[:, :], hnH[:, 2 * h + e, :],
                                            ALU.subtract).then_inc(hsem["lo"], 1)
                dve.wait_ge(hsem["cp"], h + 1)
                if h >= 2:
                    dve.wait_ge(c_out[h % 2], 32 * (h // 2))
                n0h = n0T[:, :].rearrange("p (b h) -> p b h", h=MH)[:, :, h]
                nc.vector.tensor_copy(Cp[:, h % 2, :], PS[:, 6, 0:DV])
                nc.vector.tensor_copy(nnew[:, h:h + 1], PS[:, 6, 256:257])
                link("V", dve, nc.vector.tensor_tensor(nmul[:, :], n0h, dec[:, :], ALU.mult))
                nc.vector.tensor_tensor(nnew[:, 4:36].rearrange("p (b h) -> p b h", h=MH)[:, :, h], nmul[:, :],
                                        PS[:, 6, 257:257 + NB], ALU.add).then_inc(hsem["cpi"], 1)
                for rnd, banks in enumerate(((1, 4), (5, 6))):
                    dve.wait_ge(hsem["cs"], 2 * h + rnd + 1)
                    for i in range(2):
                        for g in range(2):
                            b = 4 * g + 2 * rnd + i
                            m = nc.vector.scalar_tensor_tensor(
                                out=C0[:, h % 2, b, :], in0=C0[:, h % 2, b, :], scalar=dec[:, b:b + 1],
                                in1=PS[:, banks[g], 256 * i:256 * (i + 1)], op0=ALU.mult, op1=ALU.add)
                    m.then_inc(hsem["csi"], 1)
            dve_fm_res(dve, "mout")
            dve_norm(dve, 1, 2)
            dve_ffn(dve, 0)
            dve_norm(dve, 2, 1)

            def norm_rope(c, last):
                nh = 8 if c < 2 else 4
                x = qtok[:, :, 512 * c:512 * c + 64 * nh]
                s = sqx[:, :, 0:64 * nh]
                x4 = [qtok[:, tt, 512 * c:512 * c + 64 * nh].rearrange("p (h d) -> p h d", d=HD) for tt in range(TT)]
                nc_ = nc.vector
                dve.wait_ge(free["qkv"], TT * (c + 2))
                link("V", dve, nc_.tensor_tensor(s, x, x, ALU.mult))
                nc_.tensor_reduce(rss[:, :, 0:nh], s.rearrange("p t (h d) -> p t h d", d=HD), AX.X, ALU.add) \
                    .then_inc(asem["rss"], 1)
                yield
                dve.wait_ge(asem["rs"], c + 1)
                for tt in range(TT):
                    m = nc_.tensor_tensor(x4[tt], x4[tt], rss[:, tt, 0:nh].unsqueeze(2).to_broadcast([128, nh, HD]),
                                          ALU.mult)
                link("V", dve, m)
                yield
                w = qw[:, 0 if c < 2 else 1, :].unsqueeze(1).to_broadcast([128, nh, HD])
                for tt in range(TT):
                    m = nc_.tensor_tensor(x4[tt], x4[tt], w, ALU.mult)
                link("V", dve, m)
                yield
                for tt in range(TT):
                    lo, hi = x4[tt][:, :, 0:8], x4[tt][:, :, 8:16]
                    cs, sn = (const(t)[:, 8 * tt:8 * tt + 8].unsqueeze(1).to_broadcast([128, nh, 8])
                              for t in ("cos", "sin"))
                    for q, (u, v) in enumerate(((lo, cs), (hi, sn), (hi, cs), (lo, sn))):
                        m = nc_.tensor_tensor(rt[:, q, tt, 0:8 * nh].rearrange("p (h d) -> p h d", d=8), u, v, ALU.mult)
                link("V", dve, m)
                for tt in range(TT):
                    lo, hi = x4[tt][:, :, 0:8], x4[tt][:, :, 8:16]
                    r = [rt[:, q, tt, 0:8 * nh].rearrange("p (h d) -> p h d", d=8) for q in range(4)]
                    nc_.tensor_tensor(lo, r[0], r[1], ALU.subtract)
                    m = nc_.tensor_tensor(hi, r[2], r[3], ALU.add)
                m.then_inc(asem["rope"], 1)
                yield

            dve.wait_ge(asem["cz"], 1)
            dve.wait_ge(dKV, 16 * 5)
            dve.wait_ge(asem["kz"], 16 * TB)
            steps = iter(())
            for c in range(3):
                for u in range(4):
                    split_dve(dve, ahead(unit("qkv", c, u)))
                    next(steps, None)
                steps = norm_rope(c, c == 2)
            for _s in steps:
                pass
            for g in range(1, NTR, 2):
                tr_evac(dve, lambda o, i: nc.vector.tensor_copy(o, i), g, asem["trV"])

            def maxima(x):
                n, j = ITEMS[x]
                dve.wait_ge(asem["s"], x + 1)
                s = st[:, x % 2]
                if n >= 0:
                    lo, w = (0 if n else 128), 4
                    src = PS[:, 2 * (x % 2):2 * (x % 2) + 2, :].rearrange("p a (g k) -> p (a g) k", g=2)[:, :, lo:256]
                    sink = sinkb[:, 4 * j:4 * j + 4]
                    mx = s[:, 0, 0:4]
                else:
                    w, src, sink, mx = 1, PS[:, 2 * (x % 2), 0:KEYS], sinkr[:, :], s[:, 0, 0:1]
                link("V", dve, nc.vector.tensor_reduce(mx, src, AX.X, ALU.max))
                link("V", dve, nc.vector.scalar_tensor_tensor(out=s[:, 1, 0:w], in0=s[:, 0, 0:w], scalar=HD ** -0.5,
                                                              in1=sink, op0=ALU.mult, op1=ALU.max))
                nc.vector.tensor_scalar(s[:, 2, 0:w], s[:, 1, 0:w], -1.0, None, ALU.mult)
                nc.vector.tensor_tensor(s[:, 3, 0:w], sink, s[:, 1, 0:w], ALU.subtract).then_inc(asem["m"], 1)

            def normalise(x):
                n, j = ITEMS[x]
                s = st[:, x % 2]
                dve.wait_ge(asem["e"], x + 1)
                w = 4 if n >= 0 else 1
                link("V", dve, nc.vector.tensor_tensor(s[:, 4, 0:w], s[:, 4, 0:w], s[:, 5, 0:w], ALU.add))
                link("V", dve, nc.vector.reciprocal(s[:, 4, 0:w], s[:, 4, 0:w]))
                if n >= 0:
                    lo = 0 if n else 128
                    p = P[:, x % 2, :].rearrange("p (g k) -> p g k", g=4)[:, :, lo:256]
                    nc.vector.tensor_tensor(p, p, s[:, 4, :].unsqueeze(2).to_broadcast([128, 4, 256 - lo]),
                                            ALU.mult).then_inc(asem["p"], 1)
                else:
                    nc.vector.tensor_scalar(P[:, x % 2, 0:KEYS], P[:, x % 2, 0:KEYS], s[:, 4, 0:1], None,
                                            ALU.mult).then_inc(asem["p"], 1)

            def out_low(x):
                dve.wait_ge(asem["oh"], x + 1)
                src, cols, tiles = out_of(x)
                nc.vector.tensor_tensor(hnL[:, tiles, cols], src, hnH[:, tiles, cols],
                                        ALU.subtract).then_inc(asem["ol"], 1)

            maxima(0)
            maxima(1)
            normalise(0)
            for x in range(NI):
                n, j = ITEMS[x]
                if n >= 0:
                    dve.wait_ge(asem["t"], x + 1)
                    if x:
                        dve.wait_ge(asem["o"], x)
                    nc.vector.tensor_copy(PT[:, 1, :], PS[:, 5, :]).then_inc(asem["ptV"], 1)
                if x + 1 < NI:
                    normalise(x + 1)
                if x:
                    out_low(x - 1)
                if x + 2 < NI:
                    maxima(x + 2)
            out_low(NI - 1)
            dve_fm_res(dve, "sout")
            dve_norm(dve, 3, 3)
            dve_ffn(dve, 1)
            for tt in (1, 3):
                dve.wait_ge(ytr, tt + 1)
                nc.vector.tensor_copy(ytok[:, tt, :].rearrange("p (a b) -> p a b", a=2),
                                      PS[:, 2 * tt:2 * tt + 2, :]).then_inc(yV, 1)

        @block.sync
        def _(sp):
            def load(n, src, cols=1024):
                num, slot, _turn = n
                if not (isinstance(num, int) and num < RING):
                    sp.wait_ge(lo_ready, num - (RING - 1))
                sp.dma_start(stage[:, slot, 0:cols].rearrange("p (k c) -> p k c", k=src.shape[1]), src) \
                    .then_inc(staged[slot], 16)

            def k_major(w):
                return w.rearrange("(k p) c -> p k c", p=128)

            win, wqkv = k_major(I["w_mlstm_in"][0]), k_major(I["w_swa_qkv"][0])

            def fm(name, w, c0, first=0):
                for i in range(first):
                    for u in range(4):
                        load(unit(name, i, u), w[:, :, c0 + 512 * i + 128 * u:][:, :, 0:128])
                if first < 2:
                    with sp.Fori(first, 2) as i:
                        for u in range(4):
                            load(unit(name, i, u), w[:, :, bass.ds(i * 512 + (c0 + 128 * u), 128)])

            def tm(name, w, c0, chunks):
                with sp.Fori(0, chunks) as c:
                    for u in range(4):
                        load(unit(name, c, u), w[:, 2 * u:2 * u + 2, bass.ds(c * 512 + c0, 512)])

            def ffn(L):
                up, down = k_major(I["w_ffn_up"][L]), k_major(I["w_ffn_down"][L])
                with sp.Fori(0, KF // 2) as i:
                    for u in range(4):
                        load(unit(f"up{L}", i, u), up[:, :, bass.ds(i * 256 + (FF * (u % 2) + 128 * (u // 2)), 128)])
                with sp.Fori(0, KD) as m:
                    k0 = 0
                    for u in range(4):
                        load(unit(f"down{L}", m, u), down[:, k0:k0 + DOWN_K[u], bass.ds(m * 128, 128)],
                             128 * DOWN_K[u])
                        k0 += DOWN_K[u]

            fm("qk", win, 0, first=1)
            tm("v", win, 2 * MH * DK, 2)
            fm("o", win, 2 * MH * DK + MH * DV)
            fm("mout", k_major(I["w_mlstm_out"][0]), 0)
            ffn(0)
            tm("qkv", wqkv, 0, 3)
            fm("sout", k_major(I["w_swa_out"][0]), 0)
            ffn(1)

        @block.gpsimd
        def _(pool):
            def load(dst, src, s):
                pool.dma_start(dst, src).then_inc(s, 16)

            outs = [0]

            def store(dst, src, s=None):
                if s is None:
                    s = out_done
                    outs[0] += 1
                pool.dma_start(dst, src).then_inc(s, 16)

            for tt in range(4):
                load(xtok[:, tt, :], I["x_prompt"][0, 128 * tt:128 * (tt + 1), :], dX)
            load(xtok[0:NS, 4, :], I["x_sample"].rearrange("b t d -> (b t) d"), dX)
            load(C[:, :], I["const"][:, 0:NKEPT], dC)
            load(masks, I["const"][:, NKEPT:NCONST], dC)
            load(rowsD[0:2, :], I["norm_mix"], dRows)
            load(rowsD[2:4, :], I["norm_ffn"], dRows)
            load(rowsD[4:5, :], I["mlstm_head_norm"], dRows)
            load(rowsF[0:32, :], I["state_ffn_conv"].rearrange("l b r c -> (l b r) c"), dRows)
            pool.dma_start(rowsF[32:38, :], I["ffn_conv_w"].rearrange("l j c -> (l j) c")).then_inc(dGate, 16)
            pool.dma_start(rowsF[38:40, :], I["ffn_conv_b"]).then_inc(dRows, 16)
            nc.gpsimd.memset(gwS[:, :, :], 0.0).then_inc(gsem["w_hi"], 1)
            pool.wait_ge(gsem["w_hi"], 1)
            win = I["w_mlstm_in"][0].rearrange("(k p) c -> p k c", p=128)
            g0 = 2 * MH * DK + 2 * MH * DV
            load(gwS[:, :, 0:4], win[:, :, g0:g0 + 4], dGate)
            load(gwS[:, :, 32:36], win[:, :, g0 + 4:g0 + 8], dGate)
            load(gb[:, :], I["b_mlstm_gates"][0].rearrange("(g h) -> h g", g=2), dMisc)
            load(m0T[:, :], I["state_mlstm_m"][0].rearrange("b h -> h b"), dMisc)
            load(n0r[:, :], I["state_mlstm_n"][0].rearrange("b h d -> (b h) d"), dMisc)

            def load_c(h):
                load(C0[:, h % 2, :, :], I["state_mlstm_C"][0, :, h].rearrange("b d e -> d b e"), dC0[h % 2])
            load_c(0)
            load_c(1)
            for name in ("k", "v"):
                store(O["sample_" + name][0, :, 0:WIN - TB], I["cache_swa_" + name][0, :, TB:WIN])
            pool.wait_ge(gsem["rows"], 1)
            store(O["prompt_m"].rearrange("a b h -> h (a b)"), GB[:, SEQ - 1:SEQ], gsem["m_out"])
            store(O["sample_m"][0].rearrange("b h -> h b"),
                  GB[:, SEQ:T].rearrange("p (b t) -> p b t", t=TB)[:, :, TB - 1], gsem["m_out"])
            for h in range(MH):
                pool.wait_ge(hsem["csi"], 2 * h + 2)
                store(O["sample_C"][0, :, h].rearrange("b d e -> d b e"), C0[:, h % 2, :, :], c_out[h % 2])
                store(O["prompt_C"][0, 0, h], Cp[:, h % 2, :], c_out[h % 2])
                if h + 2 < MH:
                    pool.wait_ge(c_out[h % 2], 32 * (h // 2 + 1))
                    load_c(h + 2)
            pool.wait_ge(hsem["nin"], 1)
            store(O["prompt_n"][0, 0], nrow[0:4, :])
            store(O["sample_n"][0].rearrange("b h d -> (b h) d"), nrow[4:36, :])
            pool.wait_ge(gsem["m_out"], 32)
            pool.wait_ge(c_out[0], 64)
            pool.wait_ge(c_out[1], 64)
            pool.wait_ge(out_done, 16 * outs[0])
            pool.wait_ge(nrm[1]["lo"], 1)
            pool_ffn(pool, 0)
            pool.wait_ge(unit_used, SEG0["qkv"])
            for dst, name in ((Kc, "k"), (Vc, "v")):
                load(dst[:, :, :], I["cache_swa_" + name][0].rearrange("b j h d -> j b (h d)"), dKV)
            load(qw[:, 0, :], I["swa_q_norm"].to_broadcast([128, HD]), dKV)
            load(qw[:, 1, :], I["swa_k_norm"].to_broadcast([128, HD]), dKV)
            load(sinkb[:, :], I["swa_sinks"].to_broadcast([128, AH]), dKV)
            nc.gpsimd.memset(qtok[NS:128, 4, :], 0.0).then_inc(asem["cz"], 1)
            for t in range(TB):
                load(sinkr[t:128:TB, :], I["swa_sinks"].rearrange("a h -> h a"), asem["kz"])
            pool.wait_ge(asem["rope"], 3)
            pool.wait_ge(free["qkv"], TT * 4)
            for name, c in (("k", 1024), ("v", 1280)):
                store(O["prompt_" + name][0, 0].rearrange("t h d -> t (h d)"), qtok[:, 3, c:c + 256])
                for b in range(NB):
                    store(O["sample_" + name][0, b, WIN - TB:WIN].rearrange("t h d -> t (h d)"),
                          qtok[TB * b:TB * (b + 1), 4, c:c + 256])
            pool.wait_ge(out_done, 16 * outs[0])
            pool.wait_ge(nrm[3]["lo"], 1)
            pool_ffn(pool, 1)
            pool.wait_ge(cin, 2 * KF // 4)
            for L in range(2):
                store(O["prompt_conv"][L, 0], crow[0:2, L, :])
                store(O["sample_conv"][L].rearrange("b r c -> (b r) c"), crow[2:NCO, L, :])
            for tt in range(TT):
                pool.wait_ge((yA, yV)[tt % 2], tt // 2 + 1)
                if tt < 4:
                    store(O["y_prompt"][0, 128 * tt:128 * (tt + 1), :], ytok[:, tt, :])
                else:
                    store(O["y_sample"].rearrange("b t d -> (b t) d"), ytok[0:NS, 4, :])
            pool.wait_ge(out_done, 16 * outs[0])


def constants():
    import numpy as np
    c = np.zeros((128, NCONST), np.float32)

    def put(name, a, rows=128):
        lo, hi = COFF[name]
        c[0:rows, lo:hi] = a
    put("ident", np.eye(128))
    put("ones", 1.0)
    put("eps", EPS)
    put("sel", np.kron(np.eye(4), np.ones((1, 128))), 4)
    s, t = np.arange(128)[:, None], np.arange(128)[None, :]
    put("cmask", np.where(t >= s, 0.0, NEG))
    s, t = np.arange(NS)[:, None], np.arange(NS)[None, :]
    put("bmask", np.where((s // TB == t // TB) & (t >= s), 0.0, NEG), NS)
    put("blk", s // TB == np.arange(NB)[None, :], NS)
    pos = np.zeros((128, TT), np.float32)
    for tt in range(4):
        pos[:, tt] = 128 * tt + np.arange(128)
    pos[0:NS, 4] = PAST + np.arange(NS) % TB
    half = 8
    inv = np.float32(500000.0) ** (-np.arange(half, dtype=np.float32) * np.float32(2.0) / np.float32(16))
    ang = pos[:, :, None] * inv.astype(np.float32)[None, None, :]
    put("cos", np.cos(ang).reshape(128, -1))
    put("sin", np.sin(ang).reshape(128, -1))
    i, j = np.arange(128)[:, None], np.arange(256)[None, :]
    put("pmask", np.where((j >= i) & (j <= i + 128), 0.0, NEG))
    m = np.full((128, NB, KEYS), NEG, np.float32)
    t = np.arange(128) % TB
    for b in range(NB):
        m[:, b, 0:WIN] = np.where(np.arange(WIN)[None, :] >= t[:, None], 0.0, NEG)
        m[:, b, WIN + TB * b:WIN + TB * (b + 1)] = np.where(np.arange(TB)[None, :] <= t[:, None], 0.0, NEG)
    put("smask", m.reshape(128, -1))
    first = np.zeros(T, bool)
    first[0] = True
    first[SEQ::TB] = True
    put("keep", np.where(first, 0.0, 1.0), 4)
    put("drop", np.where(first, NEG, 0.0), 4)
    return c


_INS = ["x_prompt", "x_sample", "state_mlstm_C", "state_mlstm_n", "state_mlstm_m", "cache_swa_k", "cache_swa_v",
        "state_ffn_conv", "norm_mix", "norm_ffn", "w_mlstm_in", "b_mlstm_gates", "mlstm_head_norm", "w_mlstm_out",
        "w_swa_qkv", "swa_q_norm", "swa_k_norm", "swa_sinks", "w_swa_out", "w_ffn_up", "ffn_conv_w", "ffn_conv_b",
        "w_ffn_down"]
_OUTS = [("y_prompt", (1, SEQ, D)), ("y_sample", (NB, TB, D)),
         ("prompt_C", (1, 1, MH, DK, DV)), ("prompt_n", (1, 1, MH, DK)), ("prompt_m", (1, 1, MH)),
         ("prompt_k", (1, 1, WIN, KVH, HD)), ("prompt_v", (1, 1, WIN, KVH, HD)), ("prompt_conv", (2, 1, 2, FF)),
         ("sample_C", (1, NB, MH, DK, DV)), ("sample_n", (1, NB, MH, DK)), ("sample_m", (1, NB, MH)),
         ("sample_k", (1, NB, WIN, KVH, HD)), ("sample_v", (1, NB, WIN, KVH, HD)), ("sample_conv", (2, NB, 2, FF))]


def kernel(**inputs):
    import numpy as np
    import concourse.bacc as bacc
    from concourse.bass_utils import run_bass_kernel_spmd

    nc = bacc.Bacc("TRN2", target_bir_lowering=False, num_devices=1)
    arrays = {name: np.ascontiguousarray(inputs[name]) for name in _INS}
    arrays["const"] = constants()
    f32 = mybir.dt.float32
    I = {n: nc.dram_tensor("in_" + n, a.shape, f32, kind="ExternalInput").ap() for n, a in arrays.items()}
    O = {n: nc.dram_tensor("out_" + n, shape, f32, kind="ExternalOutput").ap() for n, shape in _OUTS}
    build(nc, I, O)
    r = run_bass_kernel_spmd(nc, [{"in_" + n: a for n, a in arrays.items()}], core_ids=[0])
    return tuple(r.results[0]["out_" + n] for n, _ in _OUTS)
```

```python
import concourse.bass as bass
from concourse import mybir
from contextlib import ExitStack

D = 1024
SEQ = 512
NB, TB = 8, 8
NS = NB * TB
T = SEQ + NS
HALF = T // 2
KD = D // 128
FF = 2816
KF = FF // 128
TT = 5
ROWS = [128, 128, 128, 128, NS]
MH, DK, DV = 4, 128, 256
AH, KVH, HD = 16, 4, 64
WIN = 128
PAST = 2048
EPS = 1e-6
WSCALE = 64.0
NEG = -1.0e30
KEYS = WIN + NS
RING = 4
GC = 2 + SEQ + NB * (2 + TB)
CC = GC - 2
NCO = 2 + NB * 2

SEGS = [("qk", 8), ("v", 8), ("o", 8), ("mout", 8), ("up0", 44), ("down0", 32),
        ("qkv", 12), ("sout", 8), ("up1", 44), ("down1", 32)]
SEG0 = {}
_n = 0
for _name, _count in SEGS:
    SEG0[_name] = _n
    _n += _count
UNITS = _n
DOWN_K = [6, 6, 5, 5]

CONST = [("ident", 128), ("ones", 128), ("eps", 1), ("sel", 4 * 128), ("cmask", 128), ("bmask", NS), ("blk", NB),
         ("cos", TT * 8), ("sin", TT * 8),
         ("pmask", 256), ("smask", NB * KEYS),
         ("keep", T), ("drop", T)]
COFF = {}
_n = 0
for _name, _count in CONST:
    COFF[_name] = (_n, _n + _count)
    _n += _count
NCONST = _n
NKEPT = COFF["pmask"][0]
NMASK = COFF["keep"][0] - NKEPT
NFIRST = COFF["sel"][0]


def build(nc, I, O):
    f32, f16, bf16 = mybir.dt.float32, mybir.dt.float16, mybir.dt.bfloat16
    ALU, ACT, AX = mybir.AluOpType, mybir.ActivationFunctionType, mybir.AxisListType
    ctx = ExitStack()
    with ctx:
        ctx.enter_context(nc.allow_non_contiguous_dma(reason="small state vectors"))

        def sb(name, shape, dt=f32, into=ctx):
            return into.enter_context(nc.sbuf_tensor(name, shape, dt))

        def sem(name):
            return ctx.enter_context(nc.semaphore(name))

        C = sb("C", [128, NKEPT])
        ident16 = sb("ident16", [128, 128], bf16)
        mask16 = sb("mask16", [128, 256 + NB * KEYS], bf16)
        xT = sb("xT", [128, KD, T])
        hnH = sb("hnH", [128, KD, T], f16)
        hnL = sb("hnL", [128, KD, T], f16)
        stage = sb("stage", [128, RING, 1024])
        wH = sb("wH", [128, RING, 1024], f16)
        wL = sb("wL", [128, RING, 1024], f16)
        pff = sb("pff", [128, KF, 40])
        pd = sb("pd", [128, KD, 5])
        convO = sb("convO", [128, 2, KF, NCO])
        sqsum = sb("sqsum", [128, T])
        sq = sb("sq", [128, T])
        rstd = sb("rstd", [128, T])
        ntmp = sb("ntmp", [128, 2, T])

        def const(name, rows=128):
            a, b = COFF[name]
            return C[0:rows, a:b]

        ident, ones, eps = const("ident"), const("ones"), const("eps")

        ph = ExitStack()
        xtok = sb("xtok", [128, TT, D], into=ph)
        rowsF = sb("rowsF", [40, FF], into=ph)
        rowsD = sb("rowsD", [5, D], into=ph)
        sq8 = sb("sq8", [128, KD, T], into=ph)
        ph.close()
        ph = ExitStack()
        qT = sb("qT", [128, MH, T], into=ph)
        kT = sb("kT", [128, MH, T], into=ph)
        vM = sb("vM", [128, TT, MH * DV], into=ph)
        so = sb("so", [128, KD, T], into=ph)
        C0 = sb("C0", [128, 2, NB, DV], into=ph)
        Cp = sb("Cp", [128, 2, DV], into=ph)
        gb = sb("gb", [4, 2], into=ph)
        m0T = sb("m0T", [4, NB], into=ph)
        n0r = sb("n0r", [32, DK], into=ph)
        n0T = sb("n0T", [128, 32], into=ph)
        R = sb("R", [4, 2 * SEQ + 3 * NS], into=ph)
        gcol = sb("gcol", [128, TT, 8], into=ph)
        kw = sb("kw", [128, 4, MH * DK], into=ph)
        kts = sb("kts", [NS, MH * DK], into=ph)
        early = ExitStack()
        gwS = sb("gwS", [128, KD, 64], into=early)
        gwH = sb("gwH", [128, KD, 64], f16, into=early)
        gwL = sb("gwL", [128, KD, 64], f16, into=early)
        FG = sb("FG", [4, T], into=early)
        GL = sb("GL", [4, T], into=early)
        GA2 = sb("GA2", [4, T], into=early)
        GM = sb("GM", [4, T], into=early)
        LI = sb("LI", [4, T], into=early)
        GB = sb("GB", [4, T], into=early)
        WS = sb("WS", [4, T], into=early)
        scanm = sb("scanm", [4, 2 * T], into=early)
        early.close()
        wbuf = sb("wbuf", [128, 2, 1280 + NS], into=ph)
        kwm = sb("kwm", [NS, NB, DK], into=ph)
        wsm = sb("wsm", [NS, NB], into=ph)
        wis = sb("wis", [128, 2, 2 * NS], into=ph)
        e1b = sb("e1b", [128, 2, SEQ], into=ph)
        qs = sb("qs", [128, 2, NS], into=ph)
        nqp = sb("nqp", [128, 2, NS], into=ph)
        dec = sb("dec", [128, NB], into=ph)
        nmul = sb("nmul", [128, NB], into=ph)
        nnew = sb("nnew", [128, 36], into=ph)
        nrow = sb("nrow", [36, DK], into=ph)
        hsA = sqsum
        hsB = sb("hsB", [128, T], into=ph)
        ph.close()
        ph = ExitStack()
        qtok = sb("qtok", [128, TT, 3 * 512], into=ph)
        sqx = sb("sqx", [128, TT, 512], into=ph)
        qTT = sb("qTT", [128, 2, 4, SEQ], into=ph)
        qS = sb("qS", [128, 2, NB, 4 * TB], into=ph)
        kTT = sb("kTT", [128, 2, T], into=ph)
        Kc = sb("Kc", [128, NB, 256], into=ph)
        Vc = sb("Vc", [128, NB, 256], into=ph)
        KcT = sb("KcT", [128, 2, NB, 128], into=ph)
        qw = sb("qw", [128, 2, HD], into=ph)
        sinkb = sb("sinkb", [128, AH], into=ph)
        sinkr = sb("sinkr", [128, 1], into=ph)
        rt = sb("rt", [128, 4, TT, 64], into=ph)
        rss = sb("rss", [128, TT, 8], into=ph)
        P = sb("P", [128, 2, 1024], into=ph)
        masks = P[:, :, :].rearrange("p a b -> p (a b)")[:, 0:NMASK]
        PT = sb("PT", [128, 2, 2, 512], into=ph)
        st = sb("st", [128, 2, 6, 4], into=ph)
        ph.close()
        ph = ExitStack()
        hH = sb("hH", [128, KF, T], f16, into=ph)
        hL = sb("hL", [128, KF, T], f16, into=ph)
        G = sb("G", [128, 2, GC], into=ph)
        acc = sb("acc", [128, 2, GC], into=ph)
        h32 = sb("h32", [128, 2, T], into=ph)
        crow = sb("crow", [NCO, 2, FF], into=ph)
        ph.close()
        ph = ExitStack()
        ytok = sb("ytok", [128, TT, D], into=ph)
        ph.close()

        PS = ctx.enter_context(nc.psum_tensor("PS", [128, 8, 512], f32))

        def pair(p):
            return PS[:, 2 * p:2 * p + 2, 0:HALF]

        def halves(ap):
            return ap.rearrange("p (a b) -> p a b", a=2)

        dI, dC, dMask = sem("dI"), sem("dC"), sem("dMask")
        dX = [sem(f"dX{tt}") for tt in range(TT)]
        dRows, dGate, dMisc = sem("dRows"), sem("dGate"), sem("dMisc")
        staged = [sem(f"staged{i}") for i in range(RING)]
        hi_ready, lo_ready, unit_used = sem("hi_ready"), sem("lo_ready"), sem("unit_used")
        x_tr = sem("x_tr")
        par_tr, par_in = sem("par_tr"), sem("par_in")
        masks_in = sem("masks_in")
        out_done = sem("out_done")
        chA, chV, chP = sem("act_chain"), sem("dve_chain"), sem("pool_chain")
        chains = {"A": 0, "V": 0, "P": 0}

        def link(which, eng, ins):
            s = {"A": chA, "V": chV, "P": chP}[which]
            chains[which] += 1
            ins.then_inc(s, 1)
            eng.wait_ge(s, chains[which])

        nrm = [{s: sem(f"norm{i}_{s}") for s in ("ps", "rs", "tmp", "hi", "lo")} for i in range(4)]
        free = {s: sem(s + "_free") for s in ("qk", "v", "o", "mout", "qkv", "sout", "down0", "down1")}
        tile_done = {s: sem(s + "_tile_done") for s in ("v", "qkv")}
        gsem = {s: sem("gate_" + s) for s in ("w_hi", "w_lo", "ps", "in", "softplus", "scans", "rows", "tr", "cols", "m_out", "kt", "kw", "kts")}
        hsem = {s: sem("head_" + s) for s in ("s", "e1", "e1b", "dt", "e", "w", "kwm", "num", "cp", "cpi", "cs",
                                              "csi", "abs", "hs", "sq", "ss", "rs", "f", "hi", "lo", "ntr", "nin")}
        dC0 = [sem("dC0a"), sem("dC0b")]
        c_out = [sem("c_outa"), sem("c_outb")]
        asem = {s: sem("attn_" + s) for s in ("rss", "rs", "rope", "tr", "trA", "trV", "s", "m", "e", "p", "t",
                                              "ptA", "ptV", "o", "oh", "ol", "cz", "kz")}
        dKV = sem("dKV")
        ff = [{s: sem(f"ffn{i}_{s}") for s in ("hist", "gate", "tail", "acc", "half", "conv",
                                               "gelu", "h32", "hH", "hL")} for i in range(2)]
        res = {s: (sem(s + "_res_x"), sem(s + "_res_sq")) for s in ("mout", "sout", "down0", "down1")}
        ctr, cin = sem("conv_out_tr"), sem("conv_out_in")
        ytr, yA, yV = sem("y_tr"), sem("y_in_act"), sem("y_in_dve")
        xV = sem("x_in_dve")
        xqA, xqV = sem("x_sq_act"), sem("x_sq_dve")
        pads = sem("pads")

        block = ctx.enter_context(nc.Block())

        def unit(name, i, u):
            n0 = SEG0[name]
            return n0 + 4 * i + u, u % RING, n0 // RING + i + u // RING

        def ahead(n):
            return n[0] + RING, n[1], n[2] + 1

        def split_act(act, n):
            num, slot, turn = n
            act.wait_ge(staged[slot], (turn + 1) * 16)
            if not (isinstance(num, int) and num < RING):
                act.wait_ge(unit_used, num - (RING - 1))
            nc.scalar.activation(wH[:, slot, :], stage[:, slot, :], ACT.Copy, scale=WSCALE).then_inc(hi_ready, 1)

        def split_dve(dve, n):
            num, slot, turn = n
            dve.wait_ge(hi_ready, num + 1)
            nc.vector.scalar_tensor_tensor(out=wL[:, slot, :], in0=stage[:, slot, :], scalar=WSCALE,
                                           in1=wH[:, slot, :], op0=ALU.mult,
                                           op1=ALU.subtract).then_inc(lo_ready, 1)

        THREE = [(0, 0), (0, 1), (1, 0)]

        def fm_unit(pe, n, ks, xs, out, first, last, k_wait=None):
            num, slot, _ = n
            pe.wait_ge(lo_ready, num + 1)
            w = (wH, wL)
            for j, k in enumerate(ks):
                if k_wait is not None:
                    k_wait(k)
                for a, b in THREE:
                    for hf in range(2):
                        m = nc.tensor.matmul(out[:, hf, :], w[a][:, slot, 128 * j:128 * (j + 1)],
                                             xs[b][:, k, HALF * hf:HALF * (hf + 1)],
                                             start=(first and j == 0 and (a, b) == THREE[0]),
                                             stop=(last and j == len(ks) - 1 and (a, b) == THREE[2]))
            m.then_inc(unit_used, 1)

        def pe_fm_seg(pe, name, ready, bank_wait=None):
            with pe.Fori(0, 2) as i:
                for u in range(4):
                    if bank_wait is not None:
                        bank_wait(u)
                    pe.wait_ge(free[name], 4 * i + u + 1)
                    fm_unit(pe, unit(name, i, u), range(KD), (hnH, hnL), pair(u), True, True,
                            k_wait=ready if u == 0 else None)

        def pe_tm_seg(pe, name, chunks, ready=None):
            with pe.Fori(0, chunks) as c:
                for u in range(4):
                    num, slot, _ = unit(name, c, u)
                    pe.wait_ge(lo_ready, num + 1)
                    for tt in range(TT):
                        if u == 0:
                            pe.wait_ge(free[name], TT * c + tt + 1)
                        rows = ROWS[tt]
                        for kk in range(2):
                            if ready is not None and tt == 0:
                                ready(2 * u + kk)
                            for a, b in THREE:
                                m = nc.tensor.matmul(
                                    PS[0:rows, tt, :], (hnH, hnL)[b][:, 2 * u + kk, 128 * tt:128 * tt + rows],
                                    (wH, wL)[a][:, slot, 512 * kk:512 * (kk + 1)],
                                    start=(u == 0 and kk == 0 and (a, b) == THREE[0]),
                                    stop=(u == 3 and kk == 1 and (a, b) == THREE[2]))
                        if tt == TT - 1:
                            m.then_inc(unit_used, 1)
                        elif u == 3:
                            m.then_inc(tile_done[name], 1)

        def tm_done(eng, name, c, tt):
            if tt < TT - 1:
                eng.wait_ge(tile_done[name], (TT - 1) * c + tt + 1)
            else:
                eng.wait_ge(unit_used, SEG0[name] + 4 * c + 4)

        def pe_norm(pe, i, summed, count):
            pe.wait_ge(summed, count)
            for hf in range(2):
                m = nc.tensor.matmul(PS[:, 6 + hf, 0:HALF], ones, sqsum[:, HALF * hf:HALF * (hf + 1)],
                                     start=True, stop=True)
            m.then_inc(nrm[i]["ps"], 1)

        def act_norm(act, i):
            act.preload_act_table_set("natural_log_exp_and_others")
            act.wait_ge(nrm[i]["ps"], 1)
            link("A", act, nc.scalar.activation(halves(rstd[:, :]), pair(3), ACT.Ln, bias=eps, scale=1.0 / D))
            nc.scalar.activation(rstd[:, :], rstd[:, :], ACT.Exp, scale=-0.5).then_inc(nrm[i]["rs"], 1)
            for k in range(KD):
                act.wait_ge(nrm[i]["tmp"], k + 1)
                nc.scalar.activation(hnH[:, k, :], ntmp[:, k % 2, :], ACT.Copy).then_inc(nrm[i]["hi"], 1)

        def dve_norm(dve, i, row):
            dve.wait_ge(nrm[i]["rs"], 1)

            def low(k):
                dve.wait_ge(nrm[i]["hi"], k + 1)
                nc.vector.tensor_tensor(hnL[:, k, :], ntmp[:, k % 2, :], hnH[:, k, :],
                                        ALU.subtract).then_inc(nrm[i]["lo"], 1)
            for k in range(KD):
                if k >= 2:
                    dve.wait_ge(nrm[i]["lo"], k - 1)
                nc.vector.scalar_tensor_tensor(out=ntmp[:, k % 2, :], in0=xT[:, k, :], scalar=pd[:, k, row:row + 1],
                                               in1=rstd[:, :], op0=ALU.mult,
                                               op1=ALU.mult).then_inc(nrm[i]["tmp"], 1)
                if k:
                    low(k - 1)
            low(KD - 1)

        def residual(dve, name, m, p):
            sx, ss = res[name]
            nc.vector.scalar_tensor_tensor(out=halves(xT[:, m, :]), in0=pair(p), scalar=1.0 / WSCALE,
                                           in1=halves(xT[:, m, :]), op0=ALU.mult, op1=ALU.add).then_inc(sx, 1)
            dve.wait_ge(sx, m + 1)
            nc.vector.tensor_tensor(sq[:, :], xT[:, m, :], xT[:, m, :], ALU.mult).then_inc(free[name], 1)
            dve.wait_ge(free[name], m + 1 + (4 if name in ("mout", "sout") else 2))
            nc.vector.tensor_tensor(sqsum[:, :], sqsum[:, :], sq[:, :], ALU.add).then_inc(ss, 1)
            dve.wait_ge(ss, m + 1)

        def dve_fm_res(dve, name):
            link("V", dve, nc.vector.memset(sqsum[:, :], 0.0))
            with dve.Fori(0, 2) as it:
                for u in range(4):
                    n = unit(name, it, u)
                    dve.wait_ge(unit_used, n[0] + 1)
                    residual(dve, name, 4 * it + u, u)
                    split_dve(dve, ahead(n))

        def act_splits(act, name, iters):
            with act.Fori(0, iters) as it:
                for u in range(4):
                    split_act(act, ahead(unit(name, it, u)))

        def pe_ffn(pe, L):
            up, down, f = f"up{L}", f"down{L}", ff[L]
            with pe.Fori(0, KF // 2) as i:
                for s in range(2):
                    pe.wait_ge(f["gate"], 2 * i + s + 1)
                    fm_unit(pe, unit(up, i, 2 * s), range(KD), (hnH, hnL), pair(2 * s), True, True,
                            k_wait=(lambda k: pe.wait_ge(nrm[2 * L + 1]["lo"], k + 1)) if s == 0 else None)
                    pe.wait_ge(f["h32"], 2 * i + s + 1)
                    fm_unit(pe, unit(up, i, 2 * s + 1), range(KD), (hnH, hnL), pair(2 * s + 1), True, True)
            pe.wait_ge(f["h32"], 2 + KF - 1)

            def two(i, name=down):
                for s in range(2):
                    pe.wait_ge(free[name], 2 * i + s + 1)
                    k0 = 0
                    for u in range(4):
                        n = SEG0[name] + 8 * i + 4 * s + u, u, None
                        fm_unit(pe, n, range(k0, k0 + DOWN_K[u]), (hH, hL), pair(s), u == 0, u == 3,
                                k_wait=(lambda k: pe.wait_ge(f["hL"], k + 3)) if s == 0 else None)
                        k0 += DOWN_K[u]
            with pe.Fori(0, 3) as i:
                two(i)
            if L == 1:
                for g in range(2 * KF // 4):
                    if g >= 4:
                        pe.wait_ge(cin, g - 3)
                    pe.wait_ge(f["tail"], KF)
                    for q in range(4):
                        lay, t = divmod(4 * g + q, KF)
                        m = nc.tensor.transpose(PS[0:NCO, 4 + g % 4, 128 * q:128 * (q + 1)],
                                                convO[:, lay, t, :], ident)
                    m.then_inc(ctr, 1)
            two(3)

        def act_ffn(act, L):
            up, down, f = f"up{L}", f"down{L}", ff[L]
            act.preload_act_table(ACT.Gelu)
            with act.Fori(0, KF // 2) as i:
                for s in range(2):
                    t = 2 * i + s
                    ng, nu = unit(up, i, 2 * s), unit(up, i, 2 * s + 1)
                    act.wait_ge(f["hist"], t + 1)
                    act.wait_ge(unit_used, ng[0] + 1)
                    ps = pair(2 * s)
                    nc.scalar.activation(G[:, s, 2:2 + HALF], ps[:, 0, :], ACT.Copy, scale=1.0 / WSCALE)
                    nc.scalar.activation(G[:, s, 2 + HALF:2 + SEQ], ps[:, 1, 0:SEQ - HALF], ACT.Copy,
                                         scale=1.0 / WSCALE)
                    nc.scalar.activation(
                        G[:, s, 2 + SEQ:GC].rearrange("p (b c) -> p b c", c=2 + TB)[:, :, 2:2 + TB],
                        ps[:, 1, SEQ - HALF:HALF].rearrange("p (b c) -> p b c", c=TB), ACT.Copy,
                        scale=1.0 / WSCALE).then_inc(f["gate"], 1)
                    act.wait_ge(f["gate"], t + 3)
                    nc.scalar.activation(acc[:, s, 0:CC], G[:, s, 2:GC], ACT.Identity, bias=pff[:, t, 38 + L:39 + L],
                                         scale=pff[:, t, 32 + 3 * L + 2:33 + 3 * L + 2]).then_inc(f["acc"], 1)
                    split_act(act, ahead(ng))
                    act.wait_ge(f["conv"], t + 3)
                    nc.scalar.activation(acc[:, s, 0:CC], acc[:, s, 0:CC], ACT.Gelu).then_inc(f["gelu"], 1)
                    split_act(act, ahead(nu))
                    act.wait_ge(f["h32"], t + 3)
                    nc.scalar.activation(hH[:, t, :], h32[:, s, :], ACT.Copy).then_inc(f["hH"], 1)
            with act.Fori(0, 3) as i:
                for u in range(8):
                    split_act(act, (SEG0[down] + 8 * i + u + RING, u % 4, (SEG0[down] + u) // 4 + 2 * i + 1))
            if L == 1:
                for g in range(2 * KF // 4):
                    act.wait_ge(ctr, g + 1)
                    nc.scalar.activation(crow[:, :, :].rearrange("p a b -> p (a b)")[:, 512 * g:512 * (g + 1)],
                                         PS[0:NCO, 4 + g % 4, :], ACT.Copy).then_inc(cin, 1)
                for u in range(4):
                    split_act(act, (SEG0[down] + 24 + u + RING, u, (SEG0[down] + 24) // 4 + 1))
            else:
                for u in range(8):
                    split_act(act, (SEG0[down] + 24 + u + RING, u % 4, (SEG0[down] + 24 + u) // 4 + 1))

        def dve_ffn(dve, L):
            up, down, f = f"up{L}", f"down{L}", ff[L]
            with dve.Fori(0, KF // 2) as i:
                for s in range(2):
                    t = 2 * i + s
                    ng, nu = unit(up, i, 2 * s), unit(up, i, 2 * s + 1)
                    dve.wait_ge(f["acc"], t + 1)
                    nc.vector.scalar_tensor_tensor(
                        out=acc[:, s, 0:CC], in0=G[:, s, 0:CC], scalar=pff[:, t, 32 + 3 * L:33 + 3 * L],
                        in1=acc[:, s, 0:CC], op0=ALU.mult, op1=ALU.add).then_inc(f["half"], 1)
                    dve.wait_ge(f["half"], t + 1)
                    nc.vector.scalar_tensor_tensor(
                        out=acc[:, s, 0:CC], in0=G[:, s, 1:1 + CC], scalar=pff[:, t, 33 + 3 * L:34 + 3 * L],
                        in1=acc[:, s, 0:CC], op0=ALU.mult, op1=ALU.add).then_inc(f["conv"], 1)
                    split_dve(dve, ahead(ng))
                    dve.wait_ge(unit_used, nu[0] + 1)
                    dve.wait_ge(f["gelu"], t + 1)
                    dve.wait_ge(f["hL"], t + 1)
                    ps = pair(2 * s + 1)
                    for out, a, b in (
                            (h32[:, s, 0:HALF], ps[:, 0, :], acc[:, s, 0:HALF]),
                            (h32[:, s, HALF:SEQ], ps[:, 1, 0:SEQ - HALF], acc[:, s, HALF:SEQ]),
                            (h32[:, s, SEQ:T].rearrange("p (b c) -> p b c", c=TB),
                             ps[:, 1, SEQ - HALF:HALF].rearrange("p (b c) -> p b c", c=TB),
                             acc[:, s, 2 + SEQ:GC].rearrange("p (b c) -> p b c", c=2 + TB)[:, :, 0:TB])):
                        last = nc.vector.scalar_tensor_tensor(out=out, in0=a, scalar=1.0 / WSCALE, in1=b,
                                                              op0=ALU.mult, op1=ALU.mult)
                    last.then_inc(f["h32"], 1)
                    split_dve(dve, ahead(nu))
                    dve.wait_ge(f["hH"], t + 1)
                    nc.vector.tensor_tensor(hL[:, t, :], h32[:, s, :], hH[:, t, :],
                                            ALU.subtract).then_inc(f["hL"], 1)
            link("V", dve, nc.vector.memset(sqsum[:, :], 0.0))

            def two(i, last):
                for s in range(2):
                    for u in range(4):
                        if last and s == 1:
                            break
                        v = 4 * s + u
                        split_dve(dve, (SEG0[down] + 8 * i + v + RING, u, None))
                    dve.wait_ge(unit_used, SEG0[down] + 8 * i + 4 * s + 4)
                    residual(dve, down, 2 * i + s, s)
            with dve.Fori(0, 3) as i:
                two(i, False)
            two(3, L == 1)

        def pool_ffn(pool, L):
            f = ff[L]
            nc.gpsimd.memset(G[:, :, 0:2], 0.0).then_inc(pads, 1)
            pool.wait_ge(pads, L + 1)
            with pool.Fori(0, KF // 2) as i:
                for s in range(2):
                    t = 2 * i + s
                    pool.wait_ge(f["conv"], t + 1)
                    nc.gpsimd.tensor_copy(
                        G[:, s, 2 + SEQ:GC].rearrange("p (b c) -> p b c", c=2 + TB)[:, :, 0:2],
                        pff[:, t, 16 * L:16 * L + 16].rearrange("p (b c) -> p b c", c=2)).then_inc(f["hist"], 1)
                    pool.wait_ge(f["gate"], t + 3)
                    nc.gpsimd.tensor_copy(convO[:, L, t, 0:2], G[:, s, SEQ:SEQ + 2])
                    nc.gpsimd.tensor_copy(
                        convO[:, L, t, 2:NCO].rearrange("p (b c) -> p b c", c=2),
                        G[:, s, 2 + SEQ:GC].rearrange("p (b c) -> p b c", c=2 + TB)[:, :, TB:TB + 2]) \
                        .then_inc(f["tail"], 1)
                    pool.wait_ge(f["tail"], t + 1)

        wcol = [0, 512, 896, 1152]
        MEMORY_BANKS = ((0, 2), (3, 7))

        TRANSPOSES = [("cache", i) for i in range(4)] + [("q", (c, tt)) for c in range(2) for tt in range(TT)] \
            + [("k", tt) for tt in range(TT)]
        NTR = len(TRANSPOSES)
        TR_ACT = [g for g in range(NTR) if g < NTR - TT or (NTR - g) % 2]
        TR_DVE = [g for g in range(NTR) if g not in TR_ACT]
        ITEMS = [(n, j) for n in range(4) for j in range(KVH)] + [(-1, b) for b in range(NB)]
        NI = len(ITEMS)
        ACT_PT = [sum(n != 0 for n, _ in ITEMS[:x + 1]) for x in range(NI)]
        DVE_PT = [sum(n >= 0 for n, _ in ITEMS[:x + 1]) for x in range(NI)]

        def tr_evac(eng, copy, g, s):
            kind, args = TRANSPOSES[g]
            eng.wait_ge(asem["tr"], g + 1)
            ps = PS[:, g % 8, :].rearrange("p (q t) -> p q t", q=4)
            if kind == "cache":
                J, b = divmod(4 * args, NB)
                m = copy(KcT[:, J, b:b + 4, :], ps)
            elif kind == "q":
                c, tt = args
                if tt < 4:
                    m = copy(qTT[:, c, :, 128 * tt:128 * (tt + 1)], ps)
                else:
                    m = copy(qS[:, c, :, :].rearrange("p b (g t) -> p g b t", t=TB),
                             ps[:, :, 0:NS].rearrange("p g (b t) -> p g b t", t=TB))
            else:
                m = copy(kTT[:, :, 128 * args:128 * args + ROWS[args]], ps[:, 0:2, 0:ROWS[args]])
            m.then_inc(s, 1)

        def out_of(x):
            n, j = ITEMS[x]
            if n >= 0:
                return (PS[:, 6 + x % 2, 0:256].rearrange("p (a q) -> p a q", a=2),
                        slice(128 * n, 128 * (n + 1)), slice(2 * j, 2 * j + 2))
            return (PS[:, 6 + x % 2, 0:64].rearrange("p (a q) -> p a q", a=KD),
                    slice(SEQ + TB * j, SEQ + TB * (j + 1)), slice(0, KD))

        @block.tensor
        def _(pe):
            def square_sums(tt):
                if tt % 2:
                    pe.wait_ge(xqV, tt // 2 + 1)
                else:
                    pe.wait_ge(xqA, tt // 2 + 1)
                lo, hi = 128 * tt, 128 * tt + ROWS[tt]
                for a, b in ((lo, min(hi, HALF)), (max(lo, HALF), hi)):
                    if a >= b:
                        continue
                    for k in range(KD):
                        m = nc.tensor.matmul(PS[:, 6 + a // HALF, a % HALF:a % HALF + b - a], ones, sq8[:, k, a:b],
                                             start=(k == 0), stop=(k == KD - 1), skip_group_check=True)
                return m

            pe.wait_ge(dI, 16)
            for tt in range(TT):
                pe.wait_ge(dX[tt], 16)
                if tt >= 3:
                    square_sums(tt - 3)
                r = ROWS[tt]
                for k in range(KD):
                    m = nc.tensor.transpose(PS[:, 2 * (tt % 3) + k // 4, 128 * (k % 4):128 * (k % 4) + r],
                                            xtok[0:r, tt, 128 * k:128 * (k + 1)], ident[0:r, 0:r])
                m.then_inc(x_tr, 1)
            for tt in range(2, TT):
                m = square_sums(tt)
            m.then_inc(nrm[0]["ps"], 1)
            pe.wait_ge(dRows, 16 * 6)
            for k in range(KD):
                nc.tensor.transpose(PS[:, 4, 5 * k:5 * (k + 1)], rowsD[:, 128 * k:128 * (k + 1)], ident[0:5, 0:5])
            for k in range(KF):
                m = nc.tensor.transpose(PS[:, 2 + k // 12, 40 * (k % 12):40 * (k % 12) + 40],
                                        rowsF[:, 128 * k:128 * (k + 1)], ident[0:40, 0:40])
            m.then_inc(par_tr, 1)

            pe.wait_ge(gsem["w_lo"], 1)
            pe.wait_ge(nrm[0]["rs"], 1)
            for k in range(KD):
                pe.wait_ge(nrm[0]["lo"], k + 1)
                for a, b in THREE:
                    for hf in range(2):
                        m = nc.tensor.matmul(PS[0:64, 6 + hf, 0:HALF], (gwH, gwL)[a][:, k, :],
                                             (hnH, hnL)[b][:, k, HALF * hf:HALF * (hf + 1)],
                                             start=(k == 0 and (a, b) == THREE[0]),
                                             stop=(k == KD - 1 and (a, b) == THREE[2]))
            m.then_inc(gsem["ps"], 1)
            pe.wait_ge(par_in, 1)
            pe_fm_seg(pe, "qk", None, lambda u: pe.wait_ge(gsem["in"], 2) if u == 3 else None)
            pe.wait_ge(free["qk"], 4 + 7)
            pe_tm_seg(pe, "v", 2)
            pe.wait_ge(dC, 16)
            pe.wait_ge(gsem["rows"], 1)
            pe.wait_ge(dMisc, 16 * 4)
            for tt in range(TT):
                r = ROWS[tt]
                for j, row in enumerate((LI, WS)):
                    nc.tensor.transpose(PS[0:r, 5, 8 * tt + 4 * j:8 * tt + 4 * j + 4],
                                        row[:, 128 * tt:128 * tt + r], ident[0:4, 0:4])
            nc.tensor.transpose(PS[:, 5, 64:96], n0r[:, :], ident[0:32, 0:32]).then_inc(gsem["tr"], 1)
            pe.wait_ge(free["qk"], 4 + 8)
            for tt in range(TT):
                if tt >= 2:
                    pe.wait_ge(gsem["kw"], tt - 1)
                r = ROWS[tt]
                for h in range(MH):
                    m = nc.tensor.transpose(PS[0:r, 6 + tt % 2, 128 * h:128 * (h + 1)],
                                            kT[:, h, 128 * tt:128 * tt + r], ident)
                m.then_inc(gsem["kt"], 1)
            pe.wait_ge(free["v"], TT + 9)

            def o_banks(u):
                if u == 2:
                    pe.wait_ge(free["v"], TT + 10)
                    pe.wait_ge(gsem["cols"], 1)
                if u == 3:
                    pe.wait_ge(gsem["kts"], 1)
            pe_fm_seg(pe, "o", None, o_banks)


            def head_scores(h):
                if h == 0:
                    pe.wait_ge(free["o"], 4 + 8)
                else:
                    pe.wait_ge(hsem["w"], h)
                if h >= 2:
                    pe.wait_ge(hsem["csi"], 2 * h - 2)
                sel = const("sel", 4)[:, 128 * h:128 * (h + 1)]
                nc.tensor.matmul(PS[:, 0, :], sel, R[:, 0:SEQ], start=True, stop=True)
                nc.tensor.matmul(PS[:, 7, 0:3 * NS], sel, R[:, 2 * SEQ:], start=True, stop=True)
                for j, (bank, c0) in enumerate(((2, 0), (3, 0), (7, 192), (3, 384))):
                    n = SEQ - 128 * j
                    nc.tensor.matmul(PS[:, bank, c0:c0 + n], kT[:, h, 128 * j:128 * (j + 1)],
                                     qT[:, h, 128 * j:SEQ], start=True, stop=True)
                nc.tensor.matmul(PS[0:NS, 7, 448:512], kT[:, h, SEQ:T], qT[:, h, SEQ:T],
                                 start=True, stop=True).then_inc(hsem["s"], 1)
                if h:
                    pe.wait_ge(hsem["e1b"], h)
                if h >= 2:
                    pe.wait_ge(hsem["hs"], h - 1)
                nc.tensor.matmul(PS[:, 1, :], sel, R[:, SEQ:2 * SEQ], start=True, stop=True).then_inc(hsem["e1"], 1)

            def head_sums(h):
                w = wbuf[:, h % 2]
                pe.wait_ge(hsem["w"], h + 1)
                if h:
                    pe.wait_ge(hsem["rs"], h)
                    pe.wait_ge(hsem["hs"], h)

                def prompt_sums(bank):
                    for j in range(4):
                        lhs = ones if bank == 6 else vM[:, j, 256 * h + 128 * (bank - 4):][:, 0:128]
                        nc.tensor.matmul(PS[:, bank, 128 * j:SEQ], lhs, w[:, wcol[j]:wcol[j] + SEQ - 128 * j],
                                         start=(j == 0), stop=(j == 3), skip_group_check=True)

                def sample_sums(e):
                    nc.tensor.matmul(PS[:, 1, NS * e:NS * (e + 1)], vM[0:NS, 4, 256 * h + 128 * e:][:, 0:128],
                                     w[0:NS, 1280:1280 + NS], start=True, stop=False, skip_group_check=True)
                    for b in range(NB):
                        nc.tensor.matmul(PS[:, 1, NS * e + TB * b:NS * e + TB * (b + 1)],
                                         C0[:, h % 2, b, 128 * e:128 * (e + 1)], qs[:, h % 2, TB * b:TB * (b + 1)],
                                         start=False, stop=(b == NB - 1), skip_group_check=True)

                prompt_sums(4)
                prompt_sums(5)
                pe.wait_ge(dC0[h % 2], 16 * (h // 2 + 1))
                pe.wait_ge(hsem["e1b"], min(h + 2, MH))
                sample_sums(0)
                prompt_sums(6)
                sample_sums(1)
                nc.tensor.matmul(PS[:, 1, 2 * NS:3 * NS], ones[0:NS, :], w[0:NS, 1280:1280 + NS],
                                 start=True, stop=False, skip_group_check=True)
                nc.tensor.matmul(PS[:, 1, 2 * NS:3 * NS], ones, nqp[:, h % 2, :], start=False, stop=True,
                                 skip_group_check=True).then_inc(hsem["num"], 1)

            def head_norm(h):
                pe.wait_ge(hsem["sq"], 2 * h + 2)
                for hf in range(2):
                    for e in range(2):
                        m = nc.tensor.matmul(PS[:, 4 + hf, 0:HALF], ones, ntmp[:, e, HALF * hf:HALF * (hf + 1)],
                                             start=(e == 0), stop=(e == 1))
                m.then_inc(hsem["ss"], 1)

            def head_memory(h):
                if h + 1 < MH:
                    pe.wait_ge(hsem["w"], h + 2)
                else:
                    pe.wait_ge(hsem["csi"], 2 * h)
                for j in range(4):
                    nc.tensor.matmul(PS[:, 7, 0:DV], kw[:, j, 128 * h:128 * (h + 1)],
                                     vM[:, j, 256 * h:256 * (h + 1)], start=(j == 0), stop=(j == 3))
                for j in range(4):
                    nc.tensor.matmul(PS[:, 7, 256:257], kw[:, j, 128 * h:128 * (h + 1)], ones[:, 0:1],
                                     start=(j == 0), stop=(j == 3))
                pe.wait_ge(hsem["kwm"], h + 1)
                nc.tensor.matmul(PS[:, 7, 257:257 + NB], kts[:, 128 * h:128 * (h + 1)], wsm[:, :],
                                 start=True, stop=True).then_inc(hsem["cp"], 1)
                for rnd, banks in enumerate(MEMORY_BANKS):
                    if rnd == 1:
                        pe.wait_ge(hsem["cpi"], h + 1)
                    for i in range(2):
                        for g in range(2):
                            b = 4 * g + 2 * rnd + i
                            m = nc.tensor.matmul(PS[:, banks[g], 256 * i:256 * (i + 1)],
                                                 kwm[32 * g:32 * (g + 1), b, :],
                                                 vM[32 * g:32 * (g + 1), 4, 256 * h:256 * (h + 1)],
                                                 start=True, stop=True)
                    m.then_inc(hsem["cs"], 1)

            head_scores(0)
            for h in range(MH):
                if h + 1 < MH:
                    head_scores(h + 1)
                head_sums(h)
                head_memory(h)
                head_norm(h)
            pe.wait_ge(hsem["csi"], 2 * MH)
            nc.tensor.transpose(PS[0:36, 7, 0:DK], nnew[:, :], ident).then_inc(hsem["ntr"], 1)
            pe_fm_seg(pe, "mout", lambda k: pe.wait_ge(hsem["lo"], k + 1),
                      lambda u: pe.wait_ge(hsem["nin"], 1) if u == 3 else None)
            pe_norm(pe, 1, res["mout"][1], KD)
            pe.wait_ge(nrm[1]["rs"], 1)
            pe_ffn(pe, 0)

            pe_norm(pe, 2, res["down0"][1], KD)
            pe_tm_seg(pe, "qkv", 3, lambda k: pe.wait_ge(nrm[2]["lo"], k + 1))
            pe.wait_ge(nrm[2]["rs"], 1)
            pe.wait_ge(free["qkv"], TT * 4)
            pe.wait_ge(dKV, 16 * 5)
            for g, (kind, args) in enumerate(TRANSPOSES):
                if g >= 8:
                    pe.wait_ge(asem["trA"], TR_ACT.index(g - 8) + 1)
                if kind == "cache":
                    for q in range(4):
                        J, b = divmod(4 * args + q, NB)
                        m = nc.tensor.transpose(PS[:, g % 8, 128 * q:128 * (q + 1)],
                                                Kc[:, b, 128 * J:128 * (J + 1)], ident)
                elif kind == "q":
                    c, tt = args
                    pe.wait_ge(asem["rope"], c + 1)
                    r = ROWS[tt]
                    for q in range(4):
                        m = nc.tensor.transpose(
                            PS[:, g % 8, 128 * q:128 * q + r],
                            qtok[0:r, tt, 512 * c + 128 * q:512 * c + 128 * (q + 1)],
                            ident[0:r, 0:r])
                else:
                    tt = args
                    pe.wait_ge(asem["rope"], 3)
                    r = ROWS[tt]
                    for J in range(2):
                        m = nc.tensor.transpose(PS[:, g % 8, 128 * J:128 * J + r],
                                                qtok[0:r, tt, 1024 + 128 * J:1024 + 128 * (J + 1)],
                                                ident[0:r, 0:r])
                m.then_inc(asem["tr"], 1)
            pe.wait_ge(asem["trA"], len(TR_ACT))
            pe.wait_ge(asem["trV"], len(TR_DVE))
            pe.wait_ge(masks_in, 1)

            def scores(x):
                if x >= 2:
                    pe.wait_ge(asem["e"], x - 1)
                n, j = ITEMS[x]
                b0 = 2 * (x % 2)
                if n >= 0:
                    J, p = divmod(j, 2)
                    lo = 0 if n else 128
                    for hp in range(2):
                        o = PS[:, b0 + hp, :].rearrange("p (g k) -> p g k", g=2)
                        nc.tensor.matmul(o[:, :, lo:256], ident16[:, :],
                                         mask16[:, lo:256].unsqueeze(1).to_broadcast([128, 2, 256 - lo]),
                                         start=True, stop=False, skip_group_check=True)
                        for g in range(2):
                            m = nc.tensor.matmul(o[:, g, lo:256],
                                                 qTT[64 * p:64 * p + 64, J, 2 * hp + g, 128 * n:128 * (n + 1)],
                                                 kTT[64 * p:64 * p + 64, J, 128 * (n - 1) + lo:128 * (n + 1)],
                                                 start=False, stop=(g == 1), skip_group_check=True)
                else:
                    b = j
                    nc.tensor.matmul(PS[:, b0, 0:KEYS], ident16[:, :],
                                     mask16[:, 256 + KEYS * b:256 + KEYS * (b + 1)], start=True, stop=False,
                                     skip_group_check=True)
                    for kv in range(KVH):
                        J, p = divmod(kv, 2)
                        q = qS[64 * p:64 * p + 64, J, b, :]
                        nc.tensor.matmul(PS[32 * kv:32 * kv + 32, b0, 0:WIN], q, KcT[64 * p:64 * p + 64, J, b, :],
                                         start=False, stop=False, skip_group_check=True)
                        m = nc.tensor.matmul(PS[32 * kv:32 * kv + 32, b0, WIN:KEYS], q,
                                             kTT[64 * p:64 * p + 64, J, SEQ:T], start=False, stop=True,
                                             skip_group_check=True)
                m.then_inc(asem["s"], 1)

            def turn(x):
                n, j = ITEMS[x]
                pe.wait_ge(asem["p"], x + 1)
                if x:
                    if ACT_PT[x - 1]:
                        pe.wait_ge(asem["ptA"], ACT_PT[x - 1])
                    pe.wait_ge(asem["ptV"], DVE_PT[x - 1])
                if n >= 0:
                    for kb in ((0, 1) if n else (1,)):
                        for g in range(4):
                            m = nc.tensor.transpose(PS[:, 4 + kb, 128 * g:128 * (g + 1)],
                                                    P[:, x % 2, 256 * g + 128 * kb:256 * g + 128 * (kb + 1)], ident)
                else:
                    nc.tensor.transpose(PS[:, 4, 0:128], P[:, x % 2, 0:128], ident)
                    m = nc.tensor.transpose(PS[0:NS, 4, 128:256], P[:, x % 2, 128:KEYS], ident)
                m.then_inc(asem["t"], 1)

            def values(x):
                n, j = ITEMS[x]
                kbs = (0, 1) if n else (1,)
                if ACT_PT[x]:
                    pe.wait_ge(asem["ptA"], ACT_PT[x])
                pe.wait_ge(asem["ptV"], DVE_PT[x])
                if x >= 2:
                    pe.wait_ge(asem["ol"], x - 1)
                ob = 6 + x % 2
                if n >= 0:
                    for r in range(2):
                        for kb in kbs:
                            m = nc.tensor.matmul(
                                PS[64 * r:64 * r + 64, ob, 0:256],
                                qtok[:, n - 1 + kb, 1280 + 64 * j:1280 + 64 * (j + 1)],
                                PT[:, x % 2, kb, :].rearrange("p (a r q) -> p r a q", r=2, q=128)[:, r],
                                start=(kb == kbs[0]), stop=(kb == 1), skip_group_check=True)
                else:
                    b = j
                    for kv in range(KVH):
                        for r in range(2):
                            o = PS[64 * r:64 * r + 64, ob, 16 * kv:16 * (kv + 1)]
                            cols = slice(32 * kv, 32 * (kv + 1))

                            def mov(a):
                                return a.rearrange("p (a r t) -> p r a t", r=2, t=TB)[:, r]
                            nc.tensor.matmul(o, Vc[:, b, 64 * kv:64 * (kv + 1)], mov(PT[:, x % 2, 0, cols]),
                                             start=True, stop=False, skip_group_check=True)
                            m = nc.tensor.matmul(o, qtok[0:NS, 4, 1280 + 64 * kv:1280 + 64 * (kv + 1)],
                                                 mov(PT[0:NS, x % 2, 0, 128 + 32 * kv:128 + 32 * (kv + 1)]),
                                                 start=False, stop=True, skip_group_check=True)
                m.then_inc(asem["o"], 1)

            scores(0)
            scores(1)
            for x in range(NI):
                if x + 2 < NI:
                    scores(x + 2)
                turn(x)
                if x:
                    values(x - 1)
            values(NI - 1)
            pe.wait_ge(asem["ol"], NI)
            pe_fm_seg(pe, "sout", None)
            pe_norm(pe, 3, res["sout"][1], KD)
            pe.wait_ge(nrm[3]["rs"], 1)
            pe_ffn(pe, 1)

            pe.wait_ge(res["down1"][0], KD)
            pe.wait_ge(cin, 2 * KF // 4)
            for tt in range(TT):
                if tt == 4:
                    pe.wait_ge(yA, 1)
                r = ROWS[tt]
                for k in range(KD):
                    m = nc.tensor.transpose(PS[0:r, 2 * (tt % 4) + k // 4, 128 * (k % 4):128 * (k % 4 + 1)],
                                            xT[:, k, 128 * tt:128 * tt + r], ident)
                m.then_inc(ytr, 1)

        @block.scalar
        def _(act):
            for s in ("qk", "o"):
                act.sem_inc(free[s], 4)
            act.sem_inc(free["qkv"], TT)
            for L in range(2):
                act.sem_inc(ff[L]["gate"], 2)
            act.wait_ge(dI, 16)
            for tt in (0, 2, 4):
                act.wait_ge(x_tr, tt + 1)
                r = ROWS[tt]
                src = PS[:, 2 * (tt % 3):2 * (tt % 3) + 2, :].rearrange("p a (k t) -> p (a k) t", t=128)[:, :, 0:r]
                nc.scalar.activation(xT[:, :, 128 * tt:128 * tt + r], src, ACT.Copy)
                nc.scalar.activation(sq8[:, :, 128 * tt:128 * tt + r], src, ACT.Square).then_inc(xqA, 1)
            split_act(act, (0, 0, 0))
            split_act(act, (1, 1, 0))
            act.wait_ge(dGate, 16 * 2)
            act.wait_ge(gsem["w_hi"], 1)
            nc.scalar.activation(gwH[:, :, :], gwS[:, :, :], ACT.Copy, scale=WSCALE).then_inc(gsem["w_hi"], 1)
            act_norm(act, 0)
            split_act(act, (2, 2, 0))
            split_act(act, (3, 3, 0))

            act.wait_ge(gsem["ps"], 1)
            act.wait_ge(dMisc, 16 * 4)
            nc.scalar.activation(halves(LI[:, :]), PS[0:4, 6:8, 0:HALF], ACT.Identity, bias=gb[:, 0:1],
                                 scale=1.0 / WSCALE).then_inc(gsem["in"], 1)
            nc.scalar.activation(halves(FG[:, :]), PS[32:36, 6:8, 0:HALF], ACT.Identity, bias=gb[:, 1:2],
                                 scale=1.0 / WSCALE).then_inc(gsem["in"], 1)
            act.wait_ge(gsem["in"], 2)
            link("A", act, nc.scalar.activation(GL[:, :], FG[:, :], ACT.Abs))
            link("A", act, nc.scalar.activation(GL[:, :], GL[:, :], ACT.Exp, scale=-1.0))
            nc.scalar.activation(GL[:, :], GL[:, :], ACT.Ln, bias=ones[0:4, 0:1]).then_inc(gsem["softplus"], 1)
            for i, scale in enumerate((1.0 / WSCALE, DK ** -0.5 / WSCALE)):
                for u in range(4):
                    n = unit("qk", i, u)
                    act.wait_ge(unit_used, n[0] + 1)
                    nc.scalar.activation(halves((qT, kT)[i][:, u, :]), pair(u), ACT.Copy, scale=scale) \
                        .then_inc(free["qk"], 1)
                    split_act(act, ahead(n))
            act.wait_ge(gsem["scans"], 1)
            nc.scalar.activation(R[:, SEQ:2 * SEQ], GB[:, 0:SEQ], ACT.Exp, scale=-1.0)
            nc.scalar.activation(R[:, 2 * SEQ + NS:2 * SEQ + 2 * NS], GB[:, SEQ:T], ACT.Exp, scale=-1.0)
            nc.scalar.activation(R[:, 2 * SEQ + 2 * NS:], R[:, 2 * SEQ + 2 * NS:], ACT.Exp)
            nc.scalar.activation(WS[:, 0:SEQ], LI[:, 0:SEQ], ACT.Exp, bias=R[:, SEQ - 1:SEQ])
            nc.scalar.activation(WS[:, SEQ:T], WS[:, SEQ:T], ACT.Exp).then_inc(gsem["rows"], 1)
            act.preload_act_table(ACT.Sigmoid)
            act_splits(act, "v", 2)
            act.wait_ge(gsem["cols"], 1)
            for j in range(4):
                act.wait_ge(gsem["kt"], j + 1)
                for h in range(MH):
                    m = nc.scalar.activation(kw[:, j, 128 * h:128 * (h + 1)], PS[:, 6 + j % 2, 128 * h:128 * (h + 1)],
                                             ACT.Copy, scale=gcol[:, j, 4 + h:5 + h])
                m.then_inc(gsem["kw"], 1)
            act.wait_ge(gsem["kt"], TT)
            nc.scalar.activation(kts[:, :], PS[0:NS, 6, :], ACT.Copy).then_inc(gsem["kts"], 1)
            with act.Fori(0, 2) as i:
                for u in range(4):
                    n = unit("o", i, u)
                    act.wait_ge(unit_used, n[0] + 1)
                    nc.scalar.activation(halves(so[:, 4 * i + u, :]), pair(u), ACT.Sigmoid, scale=1.0 / WSCALE) \
                        .then_inc(free["o"], 1)
                    split_act(act, ahead(n))

            act.preload_act_table_set("natural_log_exp_and_others")

            def head_exps(h):
                w = wbuf[:, h % 2]
                act.wait_ge(hsem["dt"], h + 1)
                for j in range(4):
                    a = gcol[:, j, h:h + 1]
                    nc.scalar.activation(w[:, wcol[j]:wcol[j] + 128], w[:, wcol[j]:wcol[j] + 128], ACT.Exp, bias=a)
                    if j < 3:
                        nc.scalar.activation(w[:, wcol[j] + 128:wcol[j] + SEQ - 128 * j],
                                             PS[:, 0, 128 * (j + 1):SEQ], ACT.Exp, bias=a)
                nc.scalar.activation(w[0:NS, 1280:1280 + NS], w[0:NS, 1280:1280 + NS], ACT.Exp,
                                     bias=gcol[0:NS, 4, h:h + 1]).then_inc(hsem["e"], 1)
                act.wait_ge(hsem["e1"], h + 1)
                nc.scalar.activation(e1b[:, h % 2, :], PS[:, 1, :], ACT.Copy).then_inc(hsem["e1b"], 1)

            act.wait_ge(gsem["m_out"], 32)
            head_exps(0)
            for h in range(MH):
                if h + 1 < MH:
                    head_exps(h + 1)
                act.wait_ge(hsem["num"], h + 1)
                nc.scalar.activation(sq[:, 0:SEQ], PS[:, 6, :], ACT.Abs)
                nc.scalar.activation(sq[:, SEQ:T], PS[:, 1, 2 * NS:3 * NS], ACT.Abs).then_inc(hsem["abs"], 1)
                act.wait_ge(hsem["hs"], h + 1)
                nc.scalar.activation(ntmp[:, 0, :], hsA[:, :], ACT.Square).then_inc(hsem["sq"], 1)
                nc.scalar.activation(ntmp[:, 1, :], hsB[:, :], ACT.Square).then_inc(hsem["sq"], 1)
                act.wait_ge(hsem["ss"], h + 1)
                link("A", act, nc.scalar.activation(halves(rstd[:, :]), PS[:, 4:6, 0:HALF], ACT.Ln, bias=eps,
                                                    scale=1.0 / DV))
                nc.scalar.activation(rstd[:, :], rstd[:, :], ACT.Exp, scale=-0.5).then_inc(hsem["rs"], 1)
                for e, hs in enumerate((hsA, hsB)):
                    act.wait_ge(hsem["f"], 2 * h + e + 1)
                    nc.scalar.activation(hnH[:, 2 * h + e, :], hs[:, :], ACT.Copy).then_inc(hsem["hi"], 1)
            act.wait_ge(hsem["ntr"], 1)
            nc.scalar.activation(nrow[:, :], PS[0:36, 7, 0:DK], ACT.Copy).then_inc(hsem["nin"], 1)
            act_splits(act, "mout", 2)
            act_norm(act, 1)
            act_ffn(act, 0)
            act_norm(act, 2)

            def rms(c):
                act.wait_ge(asem["rss"], c + 1)
                link("A", act, nc.scalar.activation(rss[:, :, :], rss[:, :, :], ACT.Ln, bias=eps, scale=1.0 / HD))
                nc.scalar.activation(rss[:, :, :], rss[:, :, :], ACT.Exp, scale=-0.5).then_inc(asem["rs"], 1)

            act.wait_ge(asem["cz"], 1)
            for c in range(3):
                for u in range(3):
                    split_act(act, ahead(unit("qkv", c, u)))
                    if c and u == 0:
                        rms(c - 1)
                for tt in range(TT):
                    tm_done(act, "qkv", c, tt)
                    src, dst = PS[0:ROWS[tt], tt, :], qtok[0:ROWS[tt], tt, 512 * c:512 * (c + 1)]
                    if c < 2:
                        src = src.rearrange("p (a g d) -> p a g d", a=2, d=HD)
                        dst = dst.rearrange("p (g a d) -> p a g d", a=2, d=HD)
                    nc.scalar.activation(dst, src, ACT.Copy, scale=1.0 / WSCALE).then_inc(free["qkv"], 1)
                split_act(act, ahead(unit("qkv", c, 3)))
            for g in TR_ACT:
                if g == 5:
                    rms(2)
                tr_evac(act, lambda o, i: nc.scalar.activation(o, i, ACT.Copy), g, asem["trA"])

            def exps(x):
                n, j = ITEMS[x]
                act.wait_ge(asem["m"], x + 1)
                s = st[:, x % 2]
                if n >= 0:
                    lo = 0 if n else 128
                    src = PS[:, 2 * (x % 2):2 * (x % 2) + 2, :].rearrange("p a b -> p (a b)")
                    for g in range(4):
                        nc.scalar.activation(P[:, x % 2, 256 * g + lo:256 * (g + 1)],
                                             src[:, 256 * g + lo:256 * (g + 1)], ACT.Exp, bias=s[:, 2, g:g + 1],
                                             scale=HD ** -0.5, accum_out=s[:, 4, g:g + 1])
                    w = 4
                else:
                    nc.scalar.activation(P[:, x % 2, 0:KEYS], PS[:, 2 * (x % 2), 0:KEYS], ACT.Exp,
                                         bias=s[:, 2, 0:1], scale=HD ** -0.5, accum_out=s[:, 4, 0:1])
                    w = 1
                nc.scalar.activation(s[:, 5, 0:w], s[:, 3, 0:w], ACT.Exp).then_inc(asem["e"], 1)

            def out_high(x):
                act.wait_ge(asem["o"], x + 1)
                src, cols, tiles = out_of(x)
                nc.scalar.activation(hnH[:, tiles, cols], src, ACT.Copy).then_inc(asem["oh"], 1)

            exps(0)
            exps(1)
            for x in range(NI):
                n, j = ITEMS[x]
                act.wait_ge(asem["t"], x + 1)
                if n != 0:
                    if x >= 2:
                        act.wait_ge(asem["o"], x - 1)
                    if n > 0:
                        nc.scalar.activation(PT[:, x % 2, 0, :], PS[:, 4, :], ACT.Copy).then_inc(asem["ptA"], 1)
                    else:
                        nc.scalar.activation(PT[:, x % 2, 0, 0:128], PS[:, 4, 0:128], ACT.Copy)
                        nc.scalar.activation(PT[0:NS, x % 2, 0, 128:256], PS[0:NS, 4, 128:256], ACT.Copy) \
                            .then_inc(asem["ptA"], 1)
                if x + 2 < NI:
                    exps(x + 2)
                if x:
                    out_high(x - 1)
            out_high(NI - 1)
            act_splits(act, "sout", 2)
            act_norm(act, 3)
            act_ffn(act, 1)
            for tt in (0, 2, 4):
                act.wait_ge(ytr, tt + 1)
                r = ROWS[tt]
                nc.scalar.activation(ytok[0:r, tt, :].rearrange("p (a b) -> p a b", a=2),
                                     PS[0:r, 2 * (tt % 4):2 * (tt % 4) + 2, :], ACT.Copy).then_inc(yA, 1)

        @block.vector
        def _(dve):
            dve.sem_inc(free["v"], TT)
            dve.sem_inc(free["mout"], 4)
            dve.sem_inc(free["sout"], 4)
            for L in range(2):
                dve.sem_inc(free[f"down{L}"], 2)
                dve.sem_inc(ff[L]["conv"], 2)
                dve.sem_inc(ff[L]["h32"], 2)
                dve.sem_inc(ff[L]["hL"], 2)
            dve.wait_ge(dI, 16)
            nc.vector.tensor_copy(ident16[:, :], ident)
            for tt in (1, 3):
                dve.wait_ge(x_tr, tt + 1)
                cols = slice(128 * tt, 128 * tt + 128)
                nc.vector.tensor_copy(xT[:, :, cols], PS[:, 2 * (tt % 3):2 * (tt % 3) + 2, :]
                                      .rearrange("p a (k t) -> p (a k) t", t=128)).then_inc(xV, 1)
                dve.wait_ge(xV, tt // 2 + 1)
                nc.vector.tensor_tensor(sq8[:, :, cols], xT[:, :, cols], xT[:, :, cols], ALU.mult).then_inc(xqV, 1)
            split_dve(dve, (0, 0, 0))
            split_dve(dve, (1, 1, 0))
            dve.wait_ge(gsem["w_hi"], 2)
            nc.vector.scalar_tensor_tensor(out=gwL[:, :, :], in0=gwS[:, :, :], scalar=WSCALE, in1=gwH[:, :, :],
                                           op0=ALU.mult, op1=ALU.subtract).then_inc(gsem["w_lo"], 1)
            dve.wait_ge(par_tr, 1)
            nc.vector.tensor_copy(pd[:, :, :].rearrange("p k r -> p (k r)"), PS[:, 4, 0:5 * KD])
            nc.vector.tensor_copy(pff[:, 0:12, :].rearrange("p k r -> p (k r)"), PS[:, 2, 0:480])
            nc.vector.tensor_copy(pff[:, 12:KF, :].rearrange("p k r -> p (k r)"), PS[:, 3, 0:400]).then_inc(par_in, 1)
            dve.wait_ge(par_in, 1)
            dve_norm(dve, 0, 0)
            split_dve(dve, (2, 2, 0))
            split_dve(dve, (3, 3, 0))

            dve.wait_ge(gsem["softplus"], 1)
            link("V", dve, nc.vector.scalar_tensor_tensor(out=GL[:, :], in0=FG[:, :], scalar=0.0, in1=GL[:, :],
                                                          op0=ALU.min, op1=ALU.subtract))
            dve.wait_ge(dMisc, 16 * 4)
            link("V", dve, nc.vector.tensor_tensor_scan(GB[:, :], scanm[:, 0:T], GL[:, :], 0.0,
                                                        ALU.mult, ALU.add))
            link("V", dve, nc.vector.tensor_tensor(LI[:, :], LI[:, :], GB[:, :], ALU.subtract))
            link("V", dve, nc.vector.tensor_copy(GA2[:, :], LI[:, :]))

            def samples(a):
                return a.rearrange("p (b t) -> p b t", t=TB)
            m0 = m0T[:, :].unsqueeze(2)
            nc.vector.tensor_scalar(GA2[:, 0:1], LI[:, 0:1], 0.0, None, ALU.max)
            link("V", dve, nc.vector.tensor_tensor(samples(GA2[:, SEQ:T])[:, :, 0:1], samples(LI[:, SEQ:T])[:, :, 0:1],
                                                   m0, ALU.max))
            link("V", dve, nc.vector.tensor_tensor_scan(GM[:, :], scanm[:, T:2 * T], GA2[:, :], 0.0,
                                                        ALU.add, ALU.max))
            nc.vector.tensor_tensor(GB[:, :], GB[:, :], GM[:, :], ALU.add)
            nc.vector.tensor_scalar(R[:, 0:SEQ], GM[:, 0:SEQ], -1.0, None, ALU.mult)
            nc.vector.tensor_scalar(R[:, 2 * SEQ:2 * SEQ + NS], GM[:, SEQ:T], -1.0, None, ALU.mult)
            nc.vector.tensor_tensor(samples(R[:, 2 * SEQ + 2 * NS:]), m0.to_broadcast([4, NB, TB]),
                                    samples(GM[:, SEQ:T]), ALU.subtract)
            nc.vector.tensor_tensor(samples(WS[:, SEQ:T]), samples(LI[:, SEQ:T]),
                                    samples(GM[:, SEQ:T])[:, :, TB - 1:TB].to_broadcast([4, NB, TB]),
                                    ALU.subtract).then_inc(gsem["scans"], 1)
            with dve.Fori(0, 2) as i:
                for u in range(4):
                    split_dve(dve, ahead(unit("qk", i, u)))
            for c in range(2):
                for u in range(3):
                    split_dve(dve, ahead(unit("v", c, u)))
                for tt in range(TT):
                    tm_done(dve, "v", c, tt)
                    nc.vector.tensor_scalar(vM[0:ROWS[tt], tt, 512 * c:512 * (c + 1)], PS[0:ROWS[tt], tt, :],
                                            1.0 / WSCALE, None, ALU.mult).then_inc(free["v"], 1)
                split_dve(dve, ahead(unit("v", c, 3)))
            dve.wait_ge(dC, 16)
            dve.wait_ge(gsem["tr"], 1)
            nc.vector.tensor_copy(gcol[:, 0:4, :].rearrange("p a b -> p (a b)"), PS[:, 5, 0:32])
            nc.vector.tensor_copy(gcol[0:NS, 4, :], PS[0:NS, 5, 32:40])
            nc.vector.tensor_copy(n0T[:, :], PS[:, 5, 64:96]).then_inc(gsem["cols"], 1)
            dve.wait_ge(gsem["cols"], 1)
            with dve.Fori(0, 2) as i:
                for u in range(4):
                    split_dve(dve, ahead(unit("o", i, u)))

            def head_weights(h):
                w, rows = wbuf[:, h % 2], wis[:, h % 2]
                dve.wait_ge(hsem["s"], h + 1)
                if h >= 2:
                    dve.wait_ge(hsem["hs"], h - 1)
                n0h = n0T[:, :].rearrange("p (b h) -> p b h", h=MH)[:, :, h:h + 1]
                for j in range(4):
                    nc.vector.tensor_tensor(w[:, wcol[j]:wcol[j] + 128], PS[:, 0, 128 * j:128 * (j + 1)],
                                            const("cmask"), ALU.add)
                nc.vector.tensor_tensor(w[0:NS, 1280:1280 + NS], PS[0:NS, 7, 0:NS], const("bmask", NS), ALU.add) \
                    .then_inc(hsem["dt"], 1)
                link("V", dve, nc.vector.tensor_copy(rows, PS[:, 7, NS:3 * NS]))
                link("V", dve, nc.vector.tensor_tensor(qs[:, h % 2, :], qT[:, h, SEQ:T], rows[:, NS:2 * NS], ALU.mult))
                nc.vector.tensor_tensor(samples(nqp[:, h % 2, :]), samples(qs[:, h % 2, :]),
                                        n0h.to_broadcast([128, NB, TB]), ALU.mult)
                dve.wait_ge(hsem["e"], h + 1)
                nc.vector.tensor_tensor(w[:, 0:512], w[:, 0:512], PS[:, 2, :], ALU.mult)
                nc.vector.tensor_tensor(w[:, 512:896], w[:, 512:896], PS[:, 3, 0:384], ALU.mult)
                nc.vector.tensor_tensor(w[:, 896:1152], w[:, 896:1152], PS[:, 7, 192:448], ALU.mult)
                nc.vector.tensor_tensor(w[:, 1152:1280], w[:, 1152:1280], PS[:, 3, 384:512], ALU.mult)
                nc.vector.tensor_tensor(w[0:NS, 1280:1280 + NS], w[0:NS, 1280:1280 + NS],
                                        PS[0:NS, 7, 448:512], ALU.mult).then_inc(hsem["w"], 1)

            def head_keys(h):
                if h:
                    dve.wait_ge(hsem["csi"], 2 * h)
                link("V", dve, nc.vector.tensor_copy(dec[:, :].unsqueeze(2),
                                                     samples(wis[:, h % 2, NS:2 * NS])[:, :, TB - 1:TB]))
                link("V", dve, nc.vector.tensor_scalar(wsm[:, :], const("blk", NS), gcol[0:NS, 4, 4 + h:5 + h], None,
                                                       ALU.mult))
                nc.vector.tensor_tensor(kwm[:, :, :], kts[:, 128 * h:128 * (h + 1)].unsqueeze(1).to_broadcast([NS, NB, DK]),
                                        wsm[:, :].unsqueeze(2).to_broadcast([NS, NB, DK]), ALU.mult) \
                    .then_inc(hsem["kwm"], 1)

            def head_outputs(h):
                dve.wait_ge(hsem["abs"], h + 1)
                dve.wait_ge(hsem["e1b"], h + 1)
                nc.vector.tensor_tensor(sq[:, 0:SEQ], sq[:, 0:SEQ], e1b[:, h % 2, :], ALU.max)
                link("V", dve, nc.vector.tensor_tensor(sq[:, SEQ:T], sq[:, SEQ:T], wis[:, h % 2, 0:NS], ALU.max))
                link("V", dve, nc.vector.reciprocal(rstd[:, :], sq[:, :]))
                for e, hs in enumerate((hsA, hsB)):
                    nc.vector.tensor_tensor(hs[:, 0:SEQ], rstd[:, 0:SEQ], PS[:, 4 + e, :], ALU.mult)
                    m = nc.vector.tensor_tensor(hs[:, SEQ:T], rstd[:, SEQ:T], PS[:, 1, NS * e:NS * (e + 1)], ALU.mult)
                m.then_inc(hsem["hs"], 1)

            def head_new_memory(h):
                dve.wait_ge(hsem["cp"], h + 1)
                if h >= 2:
                    dve.wait_ge(c_out[h % 2], 32 * (h // 2))
                n0h = n0T[:, :].rearrange("p (b h) -> p b h", h=MH)[:, :, h]
                nc.vector.tensor_copy(Cp[:, h % 2, :], PS[:, 7, 0:DV])
                nc.vector.tensor_copy(nnew[:, h:h + 1], PS[:, 7, 256:257])
                link("V", dve, nc.vector.tensor_tensor(nmul[:, :], n0h, dec[:, :], ALU.mult))
                nc.vector.tensor_tensor(nnew[:, 4:36].rearrange("p (b h) -> p b h", h=MH)[:, :, h], nmul[:, :],
                                        PS[:, 7, 257:257 + NB], ALU.add).then_inc(hsem["cpi"], 1)

            def head_new_memories(h, rnd):
                dve.wait_ge(hsem["cs"], 2 * h + rnd + 1)
                for i in range(2):
                    for g in range(2):
                        b = 4 * g + 2 * rnd + i
                        m = nc.vector.scalar_tensor_tensor(
                            out=C0[:, h % 2, b, :], in0=C0[:, h % 2, b, :], scalar=dec[:, b:b + 1],
                            in1=PS[:, MEMORY_BANKS[rnd][g], 256 * i:256 * (i + 1)], op0=ALU.mult, op1=ALU.add)
                m.then_inc(hsem["csi"], 1)

            def head_gate(h):
                dve.wait_ge(hsem["rs"], h + 1)
                for e, hs in enumerate((hsA, hsB)):
                    link("V", dve, nc.vector.scalar_tensor_tensor(out=hs[:, :], in0=hs[:, :],
                                                                  scalar=pd[:, 2 * h + e, 4:5], in1=rstd[:, :],
                                                                  op0=ALU.mult, op1=ALU.mult))
                    nc.vector.tensor_tensor(hs[:, :], hs[:, :], so[:, 2 * h + e, :], ALU.mult).then_inc(hsem["f"], 1)
                for e, hs in enumerate((hsA, hsB)):
                    dve.wait_ge(hsem["hi"], 2 * h + e + 1)
                    nc.vector.tensor_tensor(hnL[:, 2 * h + e, :], hs[:, :], hnH[:, 2 * h + e, :],
                                            ALU.subtract).then_inc(hsem["lo"], 1)

            dve.wait_ge(gsem["m_out"], 32)
            dve.wait_ge(gsem["kts"], 1)
            head_weights(0)
            for h in range(MH):
                if h + 1 < MH:
                    head_weights(h + 1)
                head_keys(h)
                head_outputs(h)
                head_new_memory(h)
                head_new_memories(h, 0)
                head_new_memories(h, 1)
                head_gate(h)
            dve.wait_ge(hsem["lo"], 2 * MH)
            dve_fm_res(dve, "mout")
            dve_norm(dve, 1, 2)
            dve_ffn(dve, 0)
            dve_norm(dve, 2, 1)

            def norm_rope(c):
                nh = 8 if c < 2 else 4
                x = qtok[:, :, 512 * c:512 * c + 64 * nh]
                s = sqx[:, :, 0:64 * nh]
                x4 = x.rearrange("p t (h d) -> p t h d", d=HD)
                nc_ = nc.vector
                dve.wait_ge(free["qkv"], TT * (c + 2))
                link("V", dve, nc_.tensor_tensor(s, x, x, ALU.mult))
                nc_.tensor_reduce(rss[:, :, 0:nh], s.rearrange("p t (h d) -> p t h d", d=HD), AX.X, ALU.add) \
                    .then_inc(asem["rss"], 1)
                yield
                dve.wait_ge(asem["rs"], c + 1)
                link("V", dve, nc_.tensor_tensor(x4, x4, rss[:, :, 0:nh].unsqueeze(3).to_broadcast([128, TT, nh, HD]),
                                                 ALU.mult))
                yield
                for tt in range(TT):
                    m = nc_.tensor_tensor(x4[:, tt], x4[:, tt],
                                          qw[:, c // 2, :].unsqueeze(1).to_broadcast([128, nh, HD]), ALU.mult)
                link("V", dve, m)
                yield
                lo, hi = x4[:, :, :, 0:8], x4[:, :, :, 8:16]
                cs, sn = (const(t).rearrange("p (t d) -> p t d", d=8).unsqueeze(2).to_broadcast([128, TT, nh, 8])
                          for t in ("cos", "sin"))
                turned = [rt[:, q, :, 0:8 * nh].rearrange("p t (h d) -> p t h d", d=8) for q in range(4)]
                for q, (u, v) in enumerate(((lo, cs), (hi, sn), (hi, cs), (lo, sn))):
                    m = nc_.tensor_tensor(turned[q], u, v, ALU.mult)
                link("V", dve, m)
                nc_.tensor_tensor(lo, turned[0], turned[1], ALU.subtract)
                m = nc_.tensor_tensor(hi, turned[2], turned[3], ALU.add)
                m.then_inc(asem["rope"], 1)
                yield

            dve.wait_ge(asem["cz"], 1)
            dve.wait_ge(dKV, 16 * 5)
            dve.wait_ge(asem["kz"], 16 * TB)
            steps = iter(())
            for c in range(3):
                for u in range(4):
                    split_dve(dve, ahead(unit("qkv", c, u)))
                    next(steps, None)
                    if u >= 2:
                        next(steps, None)
                steps = norm_rope(c)
                if c == 0:
                    dve.wait_ge(dMask, 16)
                    nc.vector.tensor_copy(mask16[:, :], masks).then_inc(masks_in, 1)
            for _s in steps:
                pass
            for g in TR_DVE:
                tr_evac(dve, lambda o, i: nc.vector.tensor_copy(o, i), g, asem["trV"])

            def maxima(x):
                n, j = ITEMS[x]
                dve.wait_ge(asem["s"], x + 1)
                s = st[:, x % 2]
                if n >= 0:
                    lo, w = (0 if n else 128), 4
                    src = PS[:, 2 * (x % 2):2 * (x % 2) + 2, :].rearrange("p a (g k) -> p (a g) k", g=2)[:, :, lo:256]
                    sink = sinkb[:, 4 * j:4 * j + 4]
                    mx = s[:, 0, 0:4]
                else:
                    w, src, sink, mx = 1, PS[:, 2 * (x % 2), 0:KEYS], sinkr[:, :], s[:, 0, 0:1]
                link("V", dve, nc.vector.tensor_reduce(mx, src, AX.X, ALU.max))
                link("V", dve, nc.vector.scalar_tensor_tensor(out=s[:, 1, 0:w], in0=s[:, 0, 0:w], scalar=HD ** -0.5,
                                                              in1=sink, op0=ALU.mult, op1=ALU.max))
                nc.vector.tensor_scalar(s[:, 2, 0:w], s[:, 1, 0:w], -1.0, None, ALU.mult)
                nc.vector.tensor_tensor(s[:, 3, 0:w], sink, s[:, 1, 0:w], ALU.subtract).then_inc(asem["m"], 1)

            def normalise(x):
                n, j = ITEMS[x]
                s = st[:, x % 2]
                dve.wait_ge(asem["e"], x + 1)
                w = 4 if n >= 0 else 1
                link("V", dve, nc.vector.tensor_tensor(s[:, 4, 0:w], s[:, 4, 0:w], s[:, 5, 0:w], ALU.add))
                link("V", dve, nc.vector.reciprocal(s[:, 4, 0:w], s[:, 4, 0:w]))
                if n >= 0:
                    lo = 0 if n else 128
                    p = P[:, x % 2, :].rearrange("p (g k) -> p g k", g=4)[:, :, lo:256]
                    nc.vector.tensor_tensor(p, p, s[:, 4, :].unsqueeze(2).to_broadcast([128, 4, 256 - lo]),
                                            ALU.mult).then_inc(asem["p"], 1)
                else:
                    nc.vector.tensor_scalar(P[:, x % 2, 0:KEYS], P[:, x % 2, 0:KEYS], s[:, 4, 0:1], None,
                                            ALU.mult).then_inc(asem["p"], 1)

            def out_low(x):
                dve.wait_ge(asem["oh"], x + 1)
                src, cols, tiles = out_of(x)
                nc.vector.tensor_tensor(hnL[:, tiles, cols], src, hnH[:, tiles, cols],
                                        ALU.subtract).then_inc(asem["ol"], 1)

            maxima(0)
            maxima(1)
            normalise(0)
            for x in range(NI):
                n, j = ITEMS[x]
                if x + 2 < NI:
                    maxima(x + 2)
                if n >= 0:
                    dve.wait_ge(asem["t"], x + 1)
                    if x >= 2:
                        dve.wait_ge(asem["o"], x - 1)
                    nc.vector.tensor_copy(PT[:, x % 2, 1, :], PS[:, 5, :]).then_inc(asem["ptV"], 1)
                if x + 1 < NI:
                    normalise(x + 1)
                if x:
                    out_low(x - 1)
            out_low(NI - 1)
            dve_fm_res(dve, "sout")
            dve_norm(dve, 3, 3)
            dve_ffn(dve, 1)
            for tt in (1, 3):
                dve.wait_ge(ytr, tt + 1)
                nc.vector.tensor_copy(ytok[:, tt, :].rearrange("p (a b) -> p a b", a=2),
                                      PS[:, 2 * tt:2 * tt + 2, :]).then_inc(yV, 1)

        @block.sync
        def _(sp):
            def load(n, src, cols=1024):
                num, slot, _turn = n
                if not (isinstance(num, int) and num < RING):
                    sp.wait_ge(lo_ready, num - (RING - 1))
                sp.dma_start(stage[:, slot, 0:cols].rearrange("p (k c) -> p k c", k=src.shape[1]), src) \
                    .then_inc(staged[slot], 16)

            def k_major(w):
                return w.rearrange("(k p) c -> p k c", p=128)

            win, wqkv = k_major(I["w_mlstm_in"][0]), k_major(I["w_swa_qkv"][0])

            def fm(name, w, c0, first=0):
                for i in range(first):
                    for u in range(4):
                        load(unit(name, i, u), w[:, :, c0 + 512 * i + 128 * u:][:, :, 0:128])
                if first < 2:
                    with sp.Fori(first, 2) as i:
                        for u in range(4):
                            load(unit(name, i, u), w[:, :, bass.ds(i * 512 + (c0 + 128 * u), 128)])

            def tm(name, w, c0, chunks):
                with sp.Fori(0, chunks) as c:
                    for u in range(4):
                        load(unit(name, c, u), w[:, 2 * u:2 * u + 2, bass.ds(c * 512 + c0, 512)])

            def ffn(L):
                up, down = k_major(I["w_ffn_up"][L]), k_major(I["w_ffn_down"][L])
                with sp.Fori(0, KF // 2) as i:
                    for u in range(4):
                        load(unit(f"up{L}", i, u), up[:, :, bass.ds(i * 256 + (FF * (u % 2) + 128 * (u // 2)), 128)])
                with sp.Fori(0, KD) as m:
                    k0 = 0
                    for u in range(4):
                        load(unit(f"down{L}", m, u), down[:, k0:k0 + DOWN_K[u], bass.ds(m * 128, 128)],
                             128 * DOWN_K[u])
                        k0 += DOWN_K[u]

            sp.dma_start(C[:, 0:NFIRST], I["const"][:, 0:NFIRST]).then_inc(dI, 16)
            for tt in range(4):
                sp.dma_start(xtok[:, tt, :], I["x_prompt"][0, 128 * tt:128 * (tt + 1), :]).then_inc(dX[tt], 16)
            sp.dma_start(xtok[0:NS, 4, :], I["x_sample"].rearrange("b t d -> (b t) d")).then_inc(dX[4], 16)
            for rows, src in ((rowsD[0:2, :], I["norm_mix"]), (rowsD[2:4, :], I["norm_ffn"]),
                              (rowsD[4:5, :], I["mlstm_head_norm"]),
                              (rowsF[0:32, :], I["state_ffn_conv"].rearrange("l b r c -> (l b r) c")),
                              (rowsF[32:38, :], I["ffn_conv_w"].rearrange("l j c -> (l j) c")),
                              (rowsF[38:40, :], I["ffn_conv_b"])):
                sp.dma_start(rows, src).then_inc(dRows, 16)
            fm("qk", win, 0, first=1)
            tm("v", win, 2 * MH * DK, 2)
            fm("o", win, 2 * MH * DK + MH * DV)
            fm("mout", k_major(I["w_mlstm_out"][0]), 0)
            ffn(0)
            tm("qkv", wqkv, 0, 3)
            fm("sout", k_major(I["w_swa_out"][0]), 0)
            ffn(1)

        @block.gpsimd
        def _(pool):
            def load(dst, src, s):
                pool.dma_start(dst, src).then_inc(s, 16)

            outs = [0]

            def store(dst, src, s=None):
                if s is None:
                    s = out_done
                    outs[0] += 1
                pool.dma_start(dst, src).then_inc(s, 16)

            nc.gpsimd.memset(gwS[:, :, :], 0.0).then_inc(gsem["w_hi"], 1)
            pool.wait_ge(gsem["w_hi"], 1)
            win = I["w_mlstm_in"][0].rearrange("(k p) c -> p k c", p=128)
            g0 = 2 * MH * DK + 2 * MH * DV
            load(gwS[:, :, 0:4], win[:, :, g0:g0 + 4], dGate)
            load(gwS[:, :, 32:36], win[:, :, g0 + 4:g0 + 8], dGate)
            load(C[:, NFIRST:NKEPT], I["const"][:, NFIRST:NKEPT], dC)
            load(gb[:, :], I["b_mlstm_gates"][0].rearrange("(g h) -> h g", g=2), dMisc)
            load(m0T[:, :], I["state_mlstm_m"][0].rearrange("b h -> h b"), dMisc)
            load(scanm[:, :], I["const"][0:4, NKEPT + NMASK:NCONST], dMisc)
            load(n0r[:, :], I["state_mlstm_n"][0].rearrange("b h d -> (b h) d"), dMisc)

            def load_c(h):
                load(C0[:, h % 2, :, :], I["state_mlstm_C"][0, :, h].rearrange("b d e -> d b e"), dC0[h % 2])
            pool.wait_ge(lo_ready, 2)
            load_c(0)
            load_c(1)
            for name in ("k", "v"):
                store(O["sample_" + name][0, :, 0:WIN - TB], I["cache_swa_" + name][0, :, TB:WIN])
            pool.wait_ge(gsem["rows"], 1)
            store(O["prompt_m"].rearrange("a b h -> h (a b)"), GB[:, SEQ - 1:SEQ], gsem["m_out"])
            store(O["sample_m"][0].rearrange("b h -> h b"),
                  GB[:, SEQ:T].rearrange("p (b t) -> p b t", t=TB)[:, :, TB - 1], gsem["m_out"])
            for h in range(MH):
                pool.wait_ge(hsem["csi"], 2 * h + 2)
                store(O["sample_C"][0, :, h].rearrange("b d e -> d b e"), C0[:, h % 2, :, :], c_out[h % 2])
                store(O["prompt_C"][0, 0, h], Cp[:, h % 2, :], c_out[h % 2])
                if h + 2 < MH:
                    pool.wait_ge(c_out[h % 2], 32 * (h // 2 + 1))
                    load_c(h + 2)
            pool.wait_ge(hsem["nin"], 1)
            store(O["prompt_n"][0, 0], nrow[0:4, :])
            store(O["sample_n"][0].rearrange("b h d -> (b h) d"), nrow[4:36, :])
            pool.wait_ge(gsem["m_out"], 32)
            pool.wait_ge(c_out[0], 64)
            pool.wait_ge(c_out[1], 64)
            pool.wait_ge(out_done, 16 * outs[0])
            pool.wait_ge(nrm[1]["lo"], 1)
            pool_ffn(pool, 0)
            pool.wait_ge(unit_used, SEG0["qkv"])
            load(masks, I["const"][:, NKEPT:NKEPT + NMASK], dMask)
            for dst, name in ((Kc, "k"), (Vc, "v")):
                load(dst[:, :, :], I["cache_swa_" + name][0].rearrange("b j h d -> j b (h d)"), dKV)
            load(qw[:, 0, :], I["swa_q_norm"].to_broadcast([128, HD]), dKV)
            load(qw[:, 1, :], I["swa_k_norm"].to_broadcast([128, HD]), dKV)
            load(sinkb[:, :], I["swa_sinks"].to_broadcast([128, AH]), dKV)
            nc.gpsimd.memset(qtok[NS:128, 4, :], 0.0).then_inc(asem["cz"], 1)
            for t in range(TB):
                load(sinkr[t:128:TB, :], I["swa_sinks"].rearrange("a h -> h a"), asem["kz"])
            pool.wait_ge(asem["rope"], 3)
            pool.wait_ge(free["qkv"], TT * 4)
            for name, c in (("k", 1024), ("v", 1280)):
                store(O["prompt_" + name][0, 0].rearrange("t h d -> t (h d)"), qtok[:, 3, c:c + 256])
                for b in range(NB):
                    store(O["sample_" + name][0, b, WIN - TB:WIN].rearrange("t h d -> t (h d)"),
                          qtok[TB * b:TB * (b + 1), 4, c:c + 256])
            pool.wait_ge(out_done, 16 * outs[0])
            pool.wait_ge(nrm[3]["lo"], 1)
            pool_ffn(pool, 1)
            pool.wait_ge(cin, 2 * KF // 4)
            for L in range(2):
                store(O["prompt_conv"][L, 0], crow[0:2, L, :])
                store(O["sample_conv"][L].rearrange("b r c -> (b r) c"), crow[2:NCO, L, :])
            for tt in range(TT):
                pool.wait_ge((yA, yV)[tt % 2], tt // 2 + 1)
                if tt < 4:
                    store(O["y_prompt"][0, 128 * tt:128 * (tt + 1), :], ytok[:, tt, :])
                else:
                    store(O["y_sample"].rearrange("b t d -> (b t) d"), ytok[0:NS, 4, :])
            pool.wait_ge(out_done, 16 * outs[0])


def constants():
    import numpy as np
    c = np.zeros((128, NCONST), np.float32)

    def put(name, a, rows=128):
        lo, hi = COFF[name]
        c[0:rows, lo:hi] = a
    put("ident", np.eye(128))
    put("ones", 1.0)
    put("eps", EPS)
    put("sel", np.kron(np.eye(4), np.ones((1, 128))), 4)
    s, t = np.arange(128)[:, None], np.arange(128)[None, :]
    put("cmask", np.where(t >= s, 0.0, NEG))
    s, t = np.arange(NS)[:, None], np.arange(NS)[None, :]
    put("bmask", np.where((s // TB == t // TB) & (t >= s), 0.0, NEG), NS)
    put("blk", s // TB == np.arange(NB)[None, :], NS)
    pos = np.zeros((128, TT), np.float32)
    for tt in range(4):
        pos[:, tt] = 128 * tt + np.arange(128)
    pos[0:NS, 4] = PAST + np.arange(NS) % TB
    half = 8
    inv = np.float32(500000.0) ** (-np.arange(half, dtype=np.float32) * np.float32(2.0) / np.float32(16))
    ang = pos[:, :, None] * inv.astype(np.float32)[None, None, :]
    put("cos", np.cos(ang).reshape(128, -1))
    put("sin", np.sin(ang).reshape(128, -1))
    i, j = np.arange(128)[:, None], np.arange(256)[None, :]
    put("pmask", np.where((j >= i) & (j <= i + 128), 0.0, NEG))
    m = np.full((128, NB, KEYS), NEG, np.float32)
    t = np.arange(128) % TB
    for b in range(NB):
        m[:, b, 0:WIN] = np.where(np.arange(WIN)[None, :] >= t[:, None], 0.0, NEG)
        m[:, b, WIN + TB * b:WIN + TB * (b + 1)] = np.where(np.arange(TB)[None, :] <= t[:, None], 0.0, NEG)
    put("smask", m.reshape(128, -1))
    first = np.zeros(T, bool)
    first[0] = True
    first[SEQ::TB] = True
    put("keep", np.where(first, 0.0, 1.0), 4)
    put("drop", np.where(first, NEG, 0.0), 4)
    return c


_INS = ["x_prompt", "x_sample", "state_mlstm_C", "state_mlstm_n", "state_mlstm_m", "cache_swa_k", "cache_swa_v",
        "state_ffn_conv", "norm_mix", "norm_ffn", "w_mlstm_in", "b_mlstm_gates", "mlstm_head_norm", "w_mlstm_out",
        "w_swa_qkv", "swa_q_norm", "swa_k_norm", "swa_sinks", "w_swa_out", "w_ffn_up", "ffn_conv_w", "ffn_conv_b",
        "w_ffn_down"]
_OUTS = [("y_prompt", (1, SEQ, D)), ("y_sample", (NB, TB, D)),
         ("prompt_C", (1, 1, MH, DK, DV)), ("prompt_n", (1, 1, MH, DK)), ("prompt_m", (1, 1, MH)),
         ("prompt_k", (1, 1, WIN, KVH, HD)), ("prompt_v", (1, 1, WIN, KVH, HD)), ("prompt_conv", (2, 1, 2, FF)),
         ("sample_C", (1, NB, MH, DK, DV)), ("sample_n", (1, NB, MH, DK)), ("sample_m", (1, NB, MH)),
         ("sample_k", (1, NB, WIN, KVH, HD)), ("sample_v", (1, NB, WIN, KVH, HD)), ("sample_conv", (2, NB, 2, FF))]


def kernel(**inputs):
    import numpy as np
    import concourse.bacc as bacc
    from concourse.bass_utils import run_bass_kernel_spmd

    nc = bacc.Bacc("TRN2", target_bir_lowering=False, num_devices=1)
    arrays = {name: np.ascontiguousarray(inputs[name]) for name in _INS}
    arrays["const"] = constants()
    f32 = mybir.dt.float32
    I = {n: nc.dram_tensor("in_" + n, a.shape, f32, kind="ExternalInput").ap() for n, a in arrays.items()}
    O = {n: nc.dram_tensor("out_" + n, shape, f32, kind="ExternalOutput").ap() for n, shape in _OUTS}
    build(nc, I, O)
    r = run_bass_kernel_spmd(nc, [{"in_" + n: a for n, a in arrays.items()}], core_ids=[0])
    return tuple(r.results[0]["out_" + n] for n, _ in _OUTS)
```
